# Optimizing a Trainium2 kernel written in Bass

```python
import math
import jax
import jax.numpy as jnp
from jax import lax
import numpy as np

D_MODEL = 1024
BATCH = 1
SEQ = 256
DEPTH = 2

N_Q_HEADS = 8
N_KV_HEADS = 2
HEAD_DIM = 64
ATT_WIDTH = N_Q_HEADS * HEAD_DIM
KV_WIDTH = N_KV_HEADS * HEAD_DIM
WINDOW = 128
BLOCK = 128
ROT_DIM = HEAD_DIM // 4
ROPE_THETA = 500000.0
CONV_WIDTH = D_MODEL - ATT_WIDTH
CONV_GROUPS = 8
CONV_K = 3
MIX_WIDTH = ATT_WIDTH + CONV_WIDTH
Q_END = ATT_WIDTH
K_END = Q_END + KV_WIDTH
V_END = K_END + KV_WIDTH
B_END = V_END + CONV_WIDTH
C_END = B_END + CONV_WIDTH
IN_WIDTH = C_END + CONV_WIDTH
D_FF_DENSE = 2816
N_EXPERTS = 8
TOP_K = 2
D_FF_EXPERT = 3584
N_DENSE = (DEPTH + 1) // 2
N_MOE = DEPTH // 2
EPS = 1e-5
NEG_INF = -1e30

kernel_name = "hybrid_swa_shortconv_moe_encoder"

def rmsnorm(x, g):
    xf = x.astype(jnp.float32)
    y = xf * lax.rsqrt(jnp.mean(xf * xf, axis=-1, keepdims=True) + EPS)
    return (y * g.astype(jnp.float32)).astype(x.dtype)

def rope_tables(positions):
    inv_freq = ROPE_THETA ** (-jnp.arange(0, ROT_DIM, 2, dtype=jnp.float32) / ROT_DIM)
    ang = positions.astype(jnp.float32)[..., None] * inv_freq
    return jnp.cos(ang)[:, :, None, :], jnp.sin(ang)[:, :, None, :]

def partial_rope(t, cos, sin):
    tf = t.astype(jnp.float32)
    x1 = tf[..., : ROT_DIM // 2]
    x2 = tf[..., ROT_DIM // 2: ROT_DIM]
    rot = jnp.concatenate([x1 * cos - x2 * sin, x2 * cos + x1 * sin], axis=-1)
    return jnp.concatenate([rot, tf[..., ROT_DIM:]], axis=-1).astype(t.dtype)

def window_attention(q, k, v, sink):
    b, s = q.shape[0], q.shape[1]
    nb = s // BLOCK
    g = N_Q_HEADS // N_KV_HEADS
    qb = q.reshape(b, nb, BLOCK, N_KV_HEADS, g, HEAD_DIM)

    def band(t):
        tp = jnp.pad(t, ((0, 0), (BLOCK, BLOCK), (0, 0), (0, 0)))
        tp = tp.reshape(b, nb + 2, BLOCK, N_KV_HEADS, HEAD_DIM)
        return jnp.concatenate([tp[:, :-2], tp[:, 1:-1], tp[:, 2:]], axis=2)

    kb, vb = band(k), band(v)
    scores = jnp.einsum('bnqkgd,bnskd->bnkgqs', qb, kb).astype(jnp.float32) * (HEAD_DIM ** -0.5)
    blk = jnp.arange(nb)[:, None, None] * BLOCK
    qpos = blk + jnp.arange(BLOCK)[None, :, None]
    kpos = blk - BLOCK + jnp.arange(3 * BLOCK)[None, None, :]
    valid = (jnp.abs(qpos - kpos) <= WINDOW) & (kpos >= 0) & (kpos < s)
    scores = jnp.where(valid[None, :, None, None], scores, NEG_INF)
    sink_b = sink.astype(jnp.float32).reshape(1, 1, N_KV_HEADS, g, 1, 1)
    m = jnp.maximum(jnp.max(scores, axis=-1, keepdims=True), sink_b)
    p = jnp.exp(scores - m)
    denom = jnp.sum(p, axis=-1, keepdims=True) + jnp.exp(sink_b - m)
    probs = (p / denom).astype(v.dtype)
    out = jnp.einsum('bnkgqs,bnskd->bnqkgd', probs, vb)
    return out.reshape(b, s, ATT_WIDTH)

def short_conv(bg, cg, u, w):
    z = cg * u
    zp = jnp.pad(z, ((0, 0), (1, 1), (0, 0)))
    conv = zp[:, :-2] * w[0] + zp[:, 1:-1] * w[1] + zp[:, 2:] * w[2]
    return bg * conv

def mixer(h, cos, sin, w_in, conv_w, sink, att_out_g, conv_out_g, w_out):
    b, s, _ = h.shape
    proj = h @ w_in
    q = proj[..., :Q_END].reshape(b, s, N_Q_HEADS, HEAD_DIM)
    k = proj[..., Q_END:K_END].reshape(b, s, N_KV_HEADS, HEAD_DIM)
    v = proj[..., K_END:V_END].reshape(b, s, N_KV_HEADS, HEAD_DIM)
    bg = proj[..., V_END:B_END]
    cg = proj[..., B_END:C_END]
    u = proj[..., C_END:]
    q = partial_rope(q, cos, sin)
    k = partial_rope(k, cos, sin)
    y_att = rmsnorm(window_attention(q, k, v, sink), att_out_g)
    y_conv = rmsnorm(short_conv(bg, cg, u, conv_w), conv_out_g)
    return jnp.concatenate([y_att, y_conv], axis=-1) @ w_out

def swiglu(t, w_gate, w_up, w_down):
    return (jax.nn.silu(t @ w_gate) * (t @ w_up)) @ w_down

def moe_swiglu(h, w_router, w_gate, w_up, w_down):
    b, s, d = h.shape
    t = h.reshape(b * s, d)
    logits = (t @ w_router).astype(jnp.float32)
    top_val, top_idx = lax.top_k(logits, TOP_K)
    gates = jax.nn.softmax(top_val, axis=-1)
    combine = jnp.sum(jax.nn.one_hot(top_idx, N_EXPERTS, dtype=jnp.float32) * gates[..., None], axis=1)
    out = jnp.zeros_like(t)
    for e in range(N_EXPERTS):
        out = out + combine[:, e:e + 1].astype(t.dtype) * swiglu(t, w_gate[e], w_up[e], w_down[e])
    return out.reshape(b, s, d)

def setup_inputs(seed: int = 0) -> dict:
    key = jax.random.key(seed)
    ks = jax.random.split(key, 20)
    f32 = jnp.float32

    def nrm(k, shape, fan_in):
        return jax.random.normal(k, shape, f32) * (fan_in ** -0.5)

    def gain(k, shape):
        return 1.0 + 0.05 * jax.random.normal(k, shape, f32)

    x = jax.random.normal(ks[0], (BATCH, SEQ, D_MODEL), f32)
    positions = jnp.broadcast_to(jnp.arange(SEQ, dtype=jnp.int32), (BATCH, SEQ))
    return {
        "x": x,
        "positions": positions,
        "mix_norm_g": gain(ks[1], (DEPTH, D_MODEL)),
        "w_in": nrm(ks[2], (DEPTH, D_MODEL, IN_WIDTH), D_MODEL),
        "conv_w": nrm(ks[3], (DEPTH, CONV_K, CONV_WIDTH), CONV_K),
        "sink": 0.5 * jax.random.normal(ks[4], (DEPTH, N_Q_HEADS), f32),
        "att_out_g": gain(ks[5], (DEPTH, ATT_WIDTH)),
        "conv_out_g": gain(ks[6], (DEPTH, CONV_WIDTH)),
        "w_out": nrm(ks[7], (DEPTH, MIX_WIDTH, D_MODEL), MIX_WIDTH),
        "ffn_norm_g": gain(ks[8], (DEPTH, D_MODEL)),
        "dense_w_gate": nrm(ks[9], (N_DENSE, D_MODEL, D_FF_DENSE), D_MODEL),
        "dense_w_up": nrm(ks[10], (N_DENSE, D_MODEL, D_FF_DENSE), D_MODEL),
        "dense_w_down": nrm(ks[11], (N_DENSE, D_FF_DENSE, D_MODEL), D_FF_DENSE),
        "router_w": nrm(ks[12], (N_MOE, D_MODEL, N_EXPERTS), D_MODEL),
        "moe_w_gate": nrm(ks[13], (N_MOE, N_EXPERTS, D_MODEL, D_FF_EXPERT), D_MODEL),
        "moe_w_up": nrm(ks[14], (N_MOE, N_EXPERTS, D_MODEL, D_FF_EXPERT), D_MODEL),
        "moe_w_down": nrm(ks[15], (N_MOE, N_EXPERTS, D_FF_EXPERT, D_MODEL), D_FF_EXPERT),
        "final_norm_g": gain(ks[16], (D_MODEL,)),
    }

def reference(x, positions, mix_norm_g, w_in, conv_w, sink, att_out_g, conv_out_g, w_out,
              ffn_norm_g, dense_w_gate, dense_w_up, dense_w_down, router_w,
              moe_w_gate, moe_w_up, moe_w_down, final_norm_g):
    cos, sin = rope_tables(positions)
    for layer in range(DEPTH):
        h = rmsnorm(x, mix_norm_g[layer])
        x = x + mixer(h, cos, sin, w_in[layer], conv_w[layer], sink[layer],
                      att_out_g[layer], conv_out_g[layer], w_out[layer])
        h = rmsnorm(x, ffn_norm_g[layer])
        j = layer // 2
        if layer % 2 == 0:
            x = x + swiglu(h, dense_w_gate[j], dense_w_up[j], dense_w_down[j])
        else:
            x = x + moe_swiglu(h, router_w[j], moe_w_gate[j], moe_w_up[j], moe_w_down[j])
    return rmsnorm(x, final_norm_g)


_drawn_inputs = setup_inputs


def setup_inputs(seed=0):
    import zlib

    import numpy as np

    out = dict(_drawn_inputs(seed))
    spreads = {}
    factors = {'sink': 6.027}
    for name, (base, spread) in spreads.items():
        noise = np.random.default_rng([zlib.crc32(name.encode()), seed]).standard_normal(out[name].shape)
        drawn = base * np.exp(spread * noise) if base else spread * noise
        out[name] = jnp.asarray(drawn.astype(out[name].dtype))
    for name, factor in factors.items():
        out[name] = (out[name] * factor).astype(out[name].dtype)
    return out
```

```python
from contextlib import ExitStack

import numpy as np

import concourse.bass as bass
from concourse import mybir

ALU = mybir.AluOpType
ACT = mybir.ActivationFunctionType
AX = mybir.AxisListType.X
F32 = mybir.dt.float32
F32R = mybir.dt.float32r
I32 = mybir.dt.int32
U32 = mybir.dt.uint32

P = 128
D = 1024
KT = D // P
SEQ = 256
NT = SEQ // P
NH, NKV, HD = 8, 2, 64
AW = NH * HD
KVW = NKV * HD
CW = D - AW
CT = CW // P
QKV = AW + 2 * KVW
ROT = HD // 4
HR = ROT // 2
WINDOW = 128
THETA = 500000.0
EPS = 1e-5
NEG = -1e30
FD = 2816
NE = 8
FE = 3584
HALF = 256
BLK = 2 * HALF
RING = 6
PW = 1024
XP = 4
DUMMY = NE + XP
NCOL = DUMMY + 1

MIX_UNITS = [("q", 4, 0, 1), ("kv", 2, 1, 1), ("c", 4, 2, 1), ("u", 4, 3, 1), ("b", 4, 0, 1),
             ("out0", 4, 1, 2), ("out1", 4, 2, 2)]
MIX_FIRST = {}
MIX_PIECES = 0
for _n, _p, _, _ in MIX_UNITS:
    MIX_FIRST[_n] = MIX_PIECES
    MIX_PIECES += _p


def gu_first(h):
    return 4 * h if h < 2 else 8 + 6 * (h - 2)


def d_first(h, halves):
    return 8 + 6 * h + 4 if h < halves - 2 else 8 + 6 * (halves - 2) + 2 * (h - halves + 2)


DH = FD // HALF
EH = FE // HALF
EB = EH // 2
D_PIECES = 6 * DH
E_PIECES = 6 * EH
MIX_BASE = [0, MIX_PIECES + D_PIECES]
DENSE_BASE = MIX_PIECES
MOE_BASE = MIX_BASE[1] + MIX_PIECES
assert E_PIECES % RING == 0


CONSTS = 10
POOL_STEPS = 6 + HR + 6


def build_trunk(nc, x_d, pos_d, mix_g, w_in, conv_w, sink, att_g, conv_g, w_out, ffn_g, dg, du, dd,
                router, eg, eu, ed, final_g, out_d):
    ctx = ExitStack()
    with ctx:
        def sb(name, shape, dt=F32):
            return ctx.enter_context(nc.sbuf_tensor(name, shape, dt))

        def sem(name):
            return ctx.enter_context(nc.semaphore(name))

        bank = [ctx.enter_context(nc.psum_tensor(f"bank{i}", [P, 512], F32)) for i in range(8)]

        raw_gu = sb("raw_gu", [P, 2, 2, KT, BLK])
        raw_d = sb("raw_d", [P, 2, 8192 // 2])
        hi = sb("hi", [P, RING, PW], F32R)
        lo = sb("lo", [P, RING, PW], F32R)
        x = sb("x", [P, NT, D])
        xn = sb("xn", [P, NT, D])
        act_hi = sb("act_hi", [P, KT, SEQ], F32R)
        act_lo = sb("act_lo", [P, KT, SEQ], F32R)
        at_hi = sb("at_hi", [P, 512], F32R)
        at_lo = sb("at_lo", [P, 512], F32R)
        gated = sb("gated", [P, 4, HALF])
        silu = sb("silu", [P, 2, HALF])
        y = sb("y", [P, D])
        gain_rows = sb("gain_rows", [P, D])
        sel = sb("sel", [P, NT, P])
        gsel = sb("gsel", [P, NT, P])
        gselT = sb("gselT", [P, SEQ])
        zeros = sb("zeros", [P, 512], F32R)
        mask = sb("mask", [P, NT, SEQ])
        ident = sb("ident", [P, P])
        ones = sb("ones", [P, P])
        before = sb("before", [P, P])
        iota = sb("iota", [P, P])
        iota8 = sb("iota8", [P, NE])
        inv_freq = sb("inv_freq", [P, HR])
        pos_i = sb("pos_i", [P, NT], I32)
        pos_f = sb("pos_f", [P, NT])
        ang = sb("ang", [P, NT, HR])
        turns = sb("turns", [P, 2, NT, HR])
        cs = sb("cs", [P, 2, NT, HR])
        eps = sb("eps", [P, 1])
        g_mix = sb("g_mix", [P, 2, KT])
        g_ffn = sb("g_ffn", [P, 2, KT])
        g_att = sb("g_att", [P, 2, 4])
        g_conv = sb("g_conv", [P, 2, CT])
        cw = sb("cw", [P, 2, 3, CT])
        sink_sb = sb("sink_sb", [P, 2, NH])
        rout = sb("rout", [P, KT, NE])
        rout_hi = sb("rout_hi", [P, KT, NE], F32R)
        rout_lo = sb("rout_lo", [P, KT, NE], F32R)
        ss = sb("ss", [P, NT])
        std = sb("std", [P, NT])
        rstd = sb("rstd", [P, NT])
        ss_a = sb("ss_a", [P, NT])
        std_a = sb("std_a", [P, NT])
        rstd_a = sb("rstd_a", [P, NT])
        mx = sb("mx", [P, NH])
        nmx = sb("nmx", [P, NT, NH])
        sinkd = sb("sinkd", [P, NT, NH])
        psums = sb("psums", [P, NT, NH])
        esink = sb("esink", [P, NT, NH])
        den = sb("den", [P, NT, NH])
        rden = sb("rden", [P, NT, NH])
        logit = sb("logit", [P, NT, NE])
        top = sb("top", [P, NT, 8])
        topi = sb("topi", [P, NT, 8], U32)
        topf = sb("topf", [P, NT, 2])
        gdiff = sb("gdiff", [P, NT])
        gexp = sb("gexp", [P, NT])
        gden = sb("gden", [P, NT])
        gates = sb("gates", [P, NT, 2])
        oneh = sb("oneh", [P, 2, NT, NE])
        chosen = sb("chosen", [P, NT, NE])
        gsum = sb("gsum", [P, 2, NT, NE])
        rank1 = sb("rank1", [P, NT, NE])
        slot_of = sb("slot_of", [P, NCOL, NT])
        gate_of = sb("gate_of", [P, NCOL, NT])
        over = sb("over", [P, 4, NE])
        xsel = sb("xsel", [P, XP, NE])
        xprod = sb("xprod", [P, XP, NT, NE])
        xid = sb("xid", [P, XP, NE])
        plan_f = sb("plan_f", [P, 8])
        plan_t = sb("plan_t", [P, 2])
        plan = sb("plan", [P, 8], I32)

        unit = [raw_gu[:, n // 2, n % 2] for n in range(4)]
        mixbuf = raw_d[:, :, :].rearrange("p a b -> p (a b)")
        prob = mixbuf[:, 0:2048]
        probT = mixbuf[:, 2048:4096]
        rope_t = mixbuf[:, 2048:2048 + 4 * NT * 10 * HR].rearrange("p (f t h j) -> p f t h j", f=4, t=NT, h=10)
        qkv = mixbuf[:, 4096:4096 + NT * QKV].rearrange("p (t n) -> p t n", t=NT)
        qT = mixbuf[:, 5632:6656].rearrange("p (c n) -> p c n", c=4)
        kT = mixbuf[:, 6656:6912]
        zT = mixbuf[:, 6912:6912 + CT * (SEQ + 2)].rearrange("p (c n) -> p c n", c=CT)
        att = qT.rearrange("p c n -> p (c n)").rearrange("p (t n) -> p t n", t=NT)
        z = xn[:, :, 0:CW]
        bb = xn[:, :, CW:D]
        yc = y[:, :].rearrange("p (c n) -> p c n", c=CT)
        sq = gated[:, :, :]
        rstd_c = silu[:, 0, :]
        std_c = silu[:, 1, :]

        unit_in = [sem(f"unit_in{n}") for n in range(4)]
        down_in = [sem(f"down_in{n}") for n in range(2)]
        hi_done, lo_done, piece_used = sem("hi_done"), sem("lo_done"), sem("piece_used")
        x_in = [sem("x_in0"), sem("x_in1")]
        consts_in = sem("consts_in")
        gain_in = sem("gain_in")
        stored = sem("stored")
        pool_done = sem("pool_done")
        dve_step, act_step = sem("dve_step"), sem("act_step")
        trig_arg = sem("trig_arg")
        trig_done = sem("trig_done")
        x_changed = sem("x_changed")
        sumsq_done, ms_done, std_done, xn_done = sem("sumsq_done"), sem("ms_done"), sem("std_done"), sem("xn_done")
        xT_done, xThi_done, xTlo_done = sem("xT_done"), sem("xThi_done"), sem("xTlo_done")
        qkv_out, rope_done = sem("qkv_out"), sem("rope_done")
        qkT_done, qT_out, kT_out = sem("qkT_done"), sem("qT_out"), sem("kT_out")
        scores_done, masked_done, exp_done, rden_done = sem("scores_done"), sem("masked_done"), sem("exp_done"), sem("rden_done")
        probT_done, probT_out_a, probT_out_v = sem("probT_done"), sem("probT_out_a"), sem("probT_out_v")
        av_done, att_done, attss_done, attms_done, attstd_done, attn_done = (
            sem("av_done"), sem("att_done"), sem("attss_done"), sem("attms_done"), sem("attstd_done"), sem("attn_done"))
        c_out, z_done, b_out, zT_done, zT_out, bT_done, yc_done, sq_done, cms_done, cstd_done, cn_done = (
            sem("c_out"), sem("z_done"), sem("b_out"), sem("zT_done"), sem("zT_out"), sem("bT_done"),
            sem("yc_done"), sem("sq_done"), sem("cms_done"), sem("cstd_done"), sem("cn_done"))
        attT_done, mixhi_done, mixlo_done = sem("attT_done"), sem("mixhi_done"), sem("mixlo_done")
        silu_done, gated_done, gT_done, atTh_done, atTl_done = (
            sem("silu_done"), sem("gated_done"), sem("gT_done"), sem("atTh_done"), sem("atTl_done"))
        routhi_done, routlo_done = sem("routhi_done"), sem("routlo_done")
        logits_done, gdiff_done, gexp_done, chosen_done, rank_done = (
            sem("logits_done"), sem("gdiff_done"), sem("gexp_done"), sem("chosen_done"), sem("rank_done"))
        plan_done = sem("plan_done")
        sel_done, gsel_done, gathered, xehi_done, xelo_done = (
            sem("sel_done"), sem("gsel_done"), sem("gathered"), sem("xehi_done"), sem("xelo_done"))
        gselT_done, gselT_out = sem("gselT_done"), sem("gselT_out")
        y_act, y_dve, scattered = sem("y_act"), sem("y_dve"), sem("scattered")
        final_done, xg_done = sem("final_done"), sem("xg_done")


        unit_seen = [[0] * 4]
        mix_landed = []
        for layer in range(2):
            seen, landed = list(unit_seen[-1]), {}
            for name, _, buf, loads in MIX_UNITS:
                seen[buf] += 16 * loads
                landed[name] = (buf, seen[buf])
            mix_landed.append(landed)
            unit_seen.append(seen)
            if layer == 0:
                unit_seen.append([n + 16 * 3 for n in seen])
        dense_seen, moe_seen = unit_seen[1], unit_seen[3]

        DOWN0 = 3 * 16

        block = ctx.enter_context(nc.Block())

        w_in_v = w_in.rearrange("l (p k) n -> l p k n", k=KT)
        w_out_v = w_out.rearrange("l (h p k) n -> l h p k n", h=2, k=4)
        dg_v = dg.rearrange("l (p k) n -> l p k n", k=KT)
        du_v = du.rearrange("l (p k) n -> l p k n", k=KT)
        dd_v = dd.rearrange("l (t p) n -> l p t n", p=P)
        eg_v = eg.rearrange("l e (p k) n -> (l e) p k n", k=KT)
        eu_v = eu.rearrange("l e (p k) n -> (l e) p k n", k=KT)
        ed_v = ed.rearrange("l e (t p) n -> (l e) p t n", p=P)
        raw_dv = raw_d[:, :, :].rearrange("p s (t n) -> p s t n", t=4)

        @block.sync
        def _(sp):
            for t in range(NT):
                sp.dma_start(x[:, t, :], x_d[0, t * P:(t + 1) * P, :]).then_inc(x_in[t], 16)

            def mixer_loads(layer):
                w = w_in_v[layer]
                base = MIX_BASE[layer]
                cols = {"q": (0, AW), "kv": (AW, QKV), "b": (QKV, QKV + CW), "c": (QKV + CW, QKV + 2 * CW),
                        "u": (QKV + 2 * CW, QKV + 3 * CW)}
                for name, _, buf, _ in MIX_UNITS:
                    if name in ("b", "out0", "out1"):
                        prev = {"b": "kv", "out0": "c", "out1": "u"}[name]
                        sp.wait_ge(lo_done, base + MIX_FIRST[prev])
                    elif layer == 1 and name in ("q", "c"):
                        h = DH - 2 if name == "q" else DH - 1
                        sp.wait_ge(lo_done, DENSE_BASE + gu_first(h) + 4)
                    if name.startswith("out"):
                        c = int(name[3])
                        for h in range(2):
                            sp.dma_start(unit[buf][:, 4 * h:4 * h + 4, :],
                                         w_out_v[layer, h, :, :, c * 512:(c + 1) * 512]).then_inc(unit_in[buf], 16)
                    else:
                        a, b = cols[name]
                        sp.dma_start(unit[buf][:, :, 0:b - a], w[:, :, a:b]).then_inc(unit_in[buf], 16)

            mixer_loads(0)
            base = MIX_BASE[0]
            blocks = (DH + 1) // 2

            def dense_down(j):
                if j < 2:
                    sp.wait_ge(mixlo_done, 8)
                else:
                    sp.wait_ge(lo_done, DENSE_BASE + d_first(2 * (j - 2) + 1, DH) + 2)
                n = min(4, 2 * (DH - 2 * j))
                sp.dma_start(raw_dv[:, j % 2, 0:n, :], dd_v[0, :, 4 * j:4 * j + n, :]).then_inc(down_in[j % 2], 16)

            for j in range(blocks):
                if j < 2:
                    sp.wait_ge(lo_done, base + [MIX_FIRST["out1"], MIX_PIECES][j])
                else:
                    sp.wait_ge(lo_done, DENSE_BASE + gu_first(2 * (j - 2) + 1) + 4)
                n = min(BLK, FD - j * BLK)
                for w, src in enumerate((dg_v, du_v)):
                    sp.dma_start(raw_gu[:, j % 2, w, :, 0:n], src[0, :, :, j * BLK:j * BLK + n])\
                        .then_inc(unit_in[2 * (j % 2) + w], 16)
                if j > 0:
                    dense_down(j - 1)
            dense_down(blocks - 1)
            mixer_loads(1)

            def expert_loads(first, e0, e1):
                for i, e in enumerate((e0, e1)):
                    for j in range(EB + 1):
                        s = (i * EB + j) % 2
                        here = first + i * E_PIECES
                        if j < EB:
                            h = 2 * j - 3
                            back = gu_first(h) + 4 if h >= 0 else gu_first(h + EH) + 4 - E_PIECES
                            sp.wait_ge(lo_done, here + back)
                            for w, src in enumerate((eg_v, eu_v)):
                                sp.dma_start(raw_gu[:, s, w, :, :], src[e, :, :, j * BLK:(j + 1) * BLK])\
                                    .then_inc(unit_in[2 * s + w], 16)
                        if j > 0:
                            h = 2 * (j - 1) - 3
                            back = d_first(h, EH) + 2 if h >= 0 else d_first(h + EH, EH) + 2 - E_PIECES
                            sp.wait_ge(lo_done, here + back)
                            sp.dma_start(raw_dv[:, 1 - s, :, :], ed_v[e, :, 4 * (j - 1):4 * j, :])\
                                .then_inc(down_in[1 - s], 16)

            sp.wait_ge(lo_done, MOE_BASE)
            sp.wait_ge(mixlo_done, 16)
            with sp.Fori(0, NE // 2) as pair:
                expert_loads(MOE_BASE + 2 * E_PIECES * pair, 2 * pair, 2 * pair + 1)
            sp.wait_ge(plan_done, 1)
            pairs = sp.value_load(plan[0:1, 5:6], min_val=0, max_val=2)
            with sp.If(pairs > 0):
                with sp.Fori(0, pairs) as pair:
                    ea = sp.value_load(plan[0:1, bass.ds(2 * pair, 1)], min_val=0, max_val=NE - 1)
                    eb = sp.value_load(plan[0:1, bass.ds(2 * pair + 1, 1)], min_val=0, max_val=NE - 1)
                    expert_loads(MOE_BASE + NE * E_PIECES + 2 * E_PIECES * pair, ea, eb)

        @block.gpsimd
        def _(pool):
            n = 0

            def link(ins):
                nonlocal n
                n += 1
                ins.then_inc(pool_done, 1)

            for t in range(NT):
                nc.gpsimd.dma_start(pos_i[:, t:t + 1], pos_d[0, t * P:(t + 1) * P].rearrange("(p o) -> p o", o=1))\
                    .then_inc(consts_in, 16)
            nc.gpsimd.dma_start(g_mix[:, :, :], mix_g.rearrange("l (p k) -> p l k", k=KT)).then_inc(consts_in, 16)
            nc.gpsimd.dma_start(g_ffn[:, :, :], ffn_g.rearrange("l (p k) -> p l k", k=KT)).then_inc(consts_in, 16)
            nc.gpsimd.dma_start(g_att[:, :, :], att_g.rearrange("l (p k) -> p l k", k=4)).then_inc(consts_in, 16)
            nc.gpsimd.dma_start(g_conv[:, :, :], conv_g.rearrange("l (p k) -> p l k", k=CT)).then_inc(consts_in, 16)
            for layer in range(2):
                nc.gpsimd.dma_start(cw[:, layer], conv_w[layer].rearrange("w (p k) -> p w k", k=CT)).then_inc(consts_in, 16)
            nc.gpsimd.dma_start(sink_sb[:, :, :], sink.partition_broadcast(P)).then_inc(consts_in, 16)
            nc.gpsimd.dma_start(rout[:, :, :], router[0].rearrange("(p k) e -> p k e", k=KT)).then_inc(consts_in, 16)
            link(nc.gpsimd.memset(ident[:, :], 0.0))
            link(nc.gpsimd.memset(ones[:, :], 1.0))
            link(nc.gpsimd.memset(mask[:, :, :], 0.0))
            link(nc.gpsimd.memset(before[:, :], 1.0))
            link(nc.gpsimd.memset(eps[:, :], EPS))
            link(nc.gpsimd.memset(zeros[:, :].bitcast(F32), 0.0))
            nc.gpsimd.memset(gselT[:, :], 0.0).then_inc(gselT_out, 1)
            freq = np.float32(THETA) ** (-np.arange(0, ROT, 2, dtype=np.float32) / np.float32(ROT))
            for j in range(HR):
                link(nc.gpsimd.memset(inv_freq[:, j:j + 1], float(freq[j])))
            pool.wait_ge(pool_done, n)
            link(nc.gpsimd.affine_select(out=ident[:, :], in_=ident[:, :], compare_op=ALU.not_equal, fill=1.0,
                                         base=0, pattern=[[-1, P]], channel_multiplier=1))
            link(nc.gpsimd.affine_select(out=mask[:, 0, :], in_=mask[:, 0, :], compare_op=ALU.is_ge, fill=NEG,
                                         base=WINDOW, pattern=[[-1, SEQ]], channel_multiplier=1))
            link(nc.gpsimd.affine_select(out=mask[:, 1, :], in_=mask[:, 1, :], compare_op=ALU.is_ge, fill=NEG,
                                         base=WINDOW - P, pattern=[[1, SEQ]], channel_multiplier=-1))
            link(nc.gpsimd.affine_select(out=before[:, :], in_=before[:, :], compare_op=ALU.is_gt, fill=0.0,
                                         base=0, pattern=[[1, P]], channel_multiplier=-1))
            link(nc.gpsimd.iota(iota[:, :], [[1, P]], base=0, channel_multiplier=0,
                                allow_small_or_imprecise_dtypes=True))
            link(nc.gpsimd.iota(iota8[:, :], [[1, NE]], base=0, channel_multiplier=0,
                                allow_small_or_imprecise_dtypes=True))
            assert n == POOL_STEPS
            nc.gpsimd.dma_start(gain_rows[:, :], ffn_g[1].partition_broadcast(P)).then_inc(gain_in, 16)
            pool.wait_ge(xg_done, 2)
            nc.gpsimd.dma_start(gain_rows[:, :], final_g.partition_broadcast(P)).then_inc(gain_in, 16)

        def wait_block_landed(eng, seen, B):
            for w in range(2):
                eng.wait_ge(unit_in[w], seen[w] + 16 + 16 * (B // 2))
                eng.wait_ge(unit_in[2 + w], seen[2 + w] + 16 * ((B + 1) // 2))

        @block.scalar
        def _(act):
            def copy(out, in_, **kw):
                return nc.scalar.activation(out, in_, ACT.Copy, **kw)

            def split_hi(n, src, ring, width=PW):
                if not isinstance(n, int) or n >= RING:
                    act.wait_ge(piece_used, n - RING + 1)
                out = hi[:, ring, 0:width]
                if len(src.shape) == 3:
                    out = out.rearrange("p (k c) -> p k c", k=src.shape[1])
                elif len(src.shape) == 4:
                    out = out.rearrange("p (k g c) -> p k g c", k=src.shape[1], g=src.shape[2])
                copy(out, src).then_inc(hi_done, 1)

            def mix_pieces(layer, a, b):
                for name, pieces, buf, _ in MIX_UNITS:
                    for q in range(pieces):
                        i = MIX_FIRST[name] + q
                        if a <= i < b:
                            if q == 0:
                                act.wait_ge(unit_in[buf], mix_landed[layer][name][1])
                            src = (unit[buf][:, 4 * q:4 * q + 4, 0:256] if name == "kv"
                                   else unit[buf][:, 2 * q:2 * q + 2, :])
                            n = MIX_BASE[layer] + i
                            split_hi(n, src, n % RING)

            def norm_stats(n, changed):
                if n == 0:
                    act.wait_ge(consts_in, 16 * CONSTS)
                    act.wait_ge(pool_done, POOL_STEPS)
                for t in range(NT):
                    if n == 0:
                        act.wait_ge(x_in[t], 16)
                    elif t == 0:
                        act.wait_ge(x_changed, changed)
                    nc.scalar.activation(xn[:, t, :], x[:, t, :], ACT.Square,
                                         accum_out=ss[:, t:t + 1]).then_inc(sumsq_done, 1)
                act.wait_ge(ms_done, n + 1)
                nc.scalar.activation(std[:, :], ss[:, :], ACT.Sqrt).then_inc(std_done, 1)

            def norm_hi(n, gain, banks):
                for b in range(4):
                    act.wait_ge(xT_done, 4 * n + b + 1)
                    for k in (2 * b, 2 * b + 1):
                        copy(act_hi[:, k, :], bank[banks[b]][:, (k % 2) * 256:(k % 2) * 256 + 256],
                             scale=gain[:, k:k + 1]).then_inc(xThi_done, 1)

            def exps(layer, t):
                act.wait_ge(masked_done, 2 * layer + t + 1)
                for h in range(NH):
                    nc.scalar.activation(prob[:, h * 256:(h + 1) * 256], prob[:, h * 256:(h + 1) * 256], ACT.Exp,
                                         bias=nmx[:, t, h:h + 1], accum_out=psums[:, t, h:h + 1]).then_inc(exp_done, 1)
                nc.scalar.activation(esink[:, t, :], sinkd[:, t, :], ACT.Exp).then_inc(exp_done, 1)

            def probT_copy(layer, t):
                act.wait_ge(probT_done, 2 * layer + t + 1)
                for b in range(2):
                    copy(probT[:, b * 512:(b + 1) * 512], bank[b][:, :]).then_inc(probT_out_a, 1)

            def mixer(layer):
                base = MIX_BASE[layer]
                pieces = lambda a, b: mix_pieces(layer, a, b)
                used = lambda i: act.wait_ge(piece_used, base + i + 1)
                if layer == 1:
                    pieces(0, 4)
                norm_stats(2 * layer, 8 * layer)
                if layer == 0:
                    act.wait_ge(trig_arg, 1)
                    nc.scalar.activation(cs[:, :, :, :], turns[:, :, :, :], ACT.Sin).then_inc(trig_done, 1)
                norm_hi(2 * layer, g_mix[:, layer, :], (0, 1, 2, 3))
                pieces(4 if layer else 0, 10)
                used(3)
                for t in range(NT):
                    copy(qkv[:, t, 0:AW].rearrange("p (c g d) -> p g c d", g=NKV, d=HD),
                         bank[4 + t][:, :].rearrange("p (g c d) -> p g c d", g=NKV, d=HD)).then_inc(qkv_out, 1)
                pieces(10, 12)
                used(5)
                for t in range(NT):
                    copy(qkv[:, t, AW:QKV], bank[6 + t][:, 0:256]).then_inc(qkv_out, 1)
                pieces(12, 14)
                used(9)
                for t in range(NT):
                    copy(z[:, t, :], bank[4 + t][:, :]).then_inc(c_out, 1)
                pieces(14, 16)
                act.wait_ge(qkT_done, layer + 1)
                for b in range(2):
                    copy(qT[:, 2 * b:2 * b + 2, :], bank[b][:, :].rearrange("p (c n) -> p c n", c=2)).then_inc(qT_out, 1)
                exps(layer, 0)
                pieces(16, 18)
                probT_copy(layer, 0)
                pieces(18, 22)
                used(17)
                for t in range(NT):
                    copy(bb[:, t, :], bank[4 + t][:, :]).then_inc(b_out, 1)
                pieces(22, 24)
                act.wait_ge(zT_done, layer + 1)
                for b in range(2):
                    copy(zT[:, 2 * b:2 * b + 2, 1:SEQ + 1],
                         bank[4 + b][:, :].rearrange("p (c n) -> p c n", c=2)).then_inc(zT_out, 1)
                exps(layer, 1)
                act.wait_ge(yc_done, layer + 1)
                nc.scalar.activation(sq, yc, ACT.Square).then_inc(sq_done, 1)
                probT_copy(layer, 1)
                for t in range(NT):
                    act.wait_ge(att_done, 2 * layer + t + 1)
                    nc.scalar.activation(prob[:, t * 512:(t + 1) * 512],
                                         att[:, t, :], ACT.Square,
                                         accum_out=ss_a[:, t:t + 1]).then_inc(attss_done, 1)
                act.wait_ge(cms_done, layer + 1)
                nc.scalar.activation(std_c, bank[2][:, 0:SEQ], ACT.Sqrt, bias=eps[:, 0:1],
                                     scale=1.0 / CW).then_inc(cstd_done, 1)
                act.wait_ge(attms_done, layer + 1)
                nc.scalar.activation(std_a[:, :], ss_a[:, :], ACT.Sqrt).then_inc(attstd_done, 1)
                act.wait_ge(cn_done, layer + 1)
                for k in range(CT):
                    copy(act_hi[:, 4 + k, :], yc[:, k, :], scale=g_conv[:, layer, k:k + 1]).then_inc(mixhi_done, 1)
                act.wait_ge(attT_done, layer + 1)
                for k in range(4):
                    copy(act_hi[:, k, :], bank[k // 2][:, (k % 2) * 256:(k % 2) * 256 + 256],
                         scale=g_att[:, layer, k:k + 1]).then_inc(mixhi_done, 1)
                pieces(24, 26)

            def gu_src(s, half, q):
                return raw_gu[:, s, :, 2 * q:2 * q + 2, half * HALF:(half + 1) * HALF].rearrange("p g k c -> p k g c")

            def down_piece_hi(first, ring, slot, half):
                for q in range(2):
                    split_hi(first + q, raw_dv[:, slot, 2 * half + q, :], (ring + q) % RING)

            def gu_pieces_hi(first, ring, slot, half):
                for q in range(4):
                    split_hi(first + q, gu_src(slot, half, q), (ring + q) % RING)

            def dense():
                b0 = DENSE_BASE

                def gu_landed(slot, count):
                    for w in range(2):
                        act.wait_ge(unit_in[2 * slot + w], dense_seen[2 * slot + w] + 16 * count)

                def silus(h, first, wait_free=True):
                    act.wait_ge(piece_used, first + 4)
                    if wait_free:
                        act.wait_ge(gated_done, h)
                    for t in range(NT):
                        ins = nc.scalar.activation(silu[:, t, :], bank[t][:, 0:HALF], ACT.Silu)
                    ins.then_inc(silu_done, 1)

                def turned(h):
                    act.wait_ge(gT_done, h + 1)
                    copy(at_hi[:, :], bank[2][:, :]).then_inc(atTh_done, 1)

                gu_landed(0, 1)
                gu_pieces_hi(b0, b0, 0, 0)
                silus(0, b0, False)
                gu_pieces_hi(b0 + 4, b0 + 4, 0, 1)
                silus(1, b0 + 4)
                with act.Fori(0, 2) as i:
                    for j in (1, 2):
                        gu_landed(j % 2, i + 1 + j // 2)
                        for half in range(2):
                            h = 4 * i + 2 * j + half
                            first = act.snap(24 * i + (b0 + gu_first(2 * j + half)))
                            gu_pieces_hi(first, b0 + gu_first(2 * j + half), j % 2, half)
                            turned(h - 2)
                            if half == 0:
                                act.wait_ge(down_in[(j - 1) % 2], 16 * i + 16)
                            down_piece_hi(first + 4, b0 + gu_first(2 * j + half) + 4, (j - 1) % 2, half)
                            silus(h, first)
                h = DH - 1
                first = b0 + gu_first(h)
                gu_landed(1, 3)
                gu_pieces_hi(first, first, 1, 0)
                turned(h - 2)
                act.wait_ge(down_in[0], 48)
                down_piece_hi(first + 4, first + 4, 0, 0)
                silus(h, first)
                turned(h - 1)
                down_piece_hi(first + 6, first + 6, 0, 1)
                turned(h)
                act.wait_ge(down_in[1], 48)
                down_piece_hi(first + 8, first + 8, 1, 0)

            def experts(passes):
                b0 = MOE_BASE

                def silu_of(half, n):
                    act.wait_ge(gated_done, n - 1)
                    nc.scalar.activation(silu[:, half, :], bank[half][:, 0:HALF], ACT.Silu).then_inc(silu_done, 1)

                def turned(half, n):
                    act.wait_ge(gT_done, n + 1)
                    copy(at_hi[:, half * 256:half * 256 + 256],
                         bank[2][:, half * 256:half * 256 + 256]).then_inc(atTh_done, 1)

                def down_landed(B):
                    act.wait_ge(down_in[0], DOWN0 + 16 + 16 * (B // 2))
                    act.wait_ge(down_in[1], DOWN0 + 16 * ((B + 1) // 2))

                def gather_hi(p):
                    act.wait_ge(gathered, p + 1)
                    for b in range(2):
                        copy(act_hi[:, 4 * b:4 * b + 4, 0:P],
                             bank[5 + b][:, :].rearrange("p (k n) -> p k n", k=4)).then_inc(xehi_done, 1)

                def rows_out(p):
                    act.wait_ge(scattered, 4 * p + 1)
                    act.wait_ge(piece_used, b0 + E_PIECES * p)
                    copy(y[:, 0:512], bank[3][:, :]).then_inc(y_act, 1)

                gather_hi(0)
                with act.Fori(0, passes) as p:
                    first = act.snap(b0 + E_PIECES * p)
                    n0 = act.snap(DH + EH * p)
                    B0 = act.snap(EB * p)
                    s0 = act.snap(p % 2)
                    wait_block_landed(act, moe_seen, B0)
                    gu_pieces_hi(first, b0, s0, 0)
                    rows_out(p)
                    gu_pieces_hi(first + 4, b0 + 4, s0, 1)
                    act.wait_ge(piece_used, first + 4)
                    silu_of(0, n0)
                    with act.Fori(1, EB) as j:
                        f = act.snap(first + 12 * j - 4)
                        n = act.snap(n0 + 2 * j)
                        B = act.snap(B0 + j)
                        s = act.snap(B % 2)
                        wait_block_landed(act, moe_seen, B)
                        gu_pieces_hi(f, b0 + 8, s, 0)
                        turned(0, n - 2)
                        silu_of(1, n - 1)
                        down_landed(B - 1)
                        down_piece_hi(f + 4, b0 + 12, 1 - s, 0)
                        gu_pieces_hi(f + 6, b0 + 14, s, 1)
                        turned(1, n - 1)
                        silu_of(0, n)
                        down_piece_hi(f + 10, b0 + 18, 1 - s, 1)
                    f = act.snap(first + d_first(EH - 2, EH))
                    n = act.snap(n0 + EH)
                    turned(0, n - 2)
                    silu_of(1, n - 1)
                    down_landed(B0 + EB - 1)
                    down_piece_hi(f, b0 + 8, s0, 0)
                    gather_hi(p + 1)
                    act.wait_ge(gselT_done, p + 1)
                    copy(gselT[:, :], bank[7][:, 0:SEQ]).then_inc(gselT_out, 1)
                    turned(1, n - 1)
                    down_piece_hi(f + 2, b0 + 10, s0, 1)
                rows_out(passes)

            mixer(0)
            norm_stats(1, 4)
            norm_hi(1, g_ffn[:, 0, :], (3, 4, 5, 6))
            dense()
            mixer(1)
            norm_stats(3, 12)
            copy(rout_hi[:, :, :], rout[:, :, :]).then_inc(routhi_done, 1)
            norm_hi(3, g_ffn[:, 1, :], (3, 4, 5, 6))
            act.wait_ge(gdiff_done, 1)
            nc.scalar.activation(gexp[:, :], gdiff[:, :], ACT.Exp).then_inc(gexp_done, 1)
            act.wait_ge(plan_done, 1)
            passes = act.value_load(plan[0:1, 4:5], min_val=NE, max_val=NE + XP)
            experts(passes)
            act.wait_ge(x_changed, 12 + 4 * (passes + 1))
            for t in range(NT):
                nc.scalar.activation(xn[:, t, :], x[:, t, :], ACT.Square,
                                     accum_out=ss[:, t:t + 1]).then_inc(sumsq_done, 1)
            act.wait_ge(ms_done, 5)
            nc.scalar.activation(std[:, :], ss[:, :], ACT.Sqrt).then_inc(std_done, 1)
            for t in range(NT):
                act.wait_ge(final_done, t + 1)
                nc.scalar.dma_start(out_d[0, t * P:(t + 1) * P, :], xn[:, t, :]).then_inc(stored, 16)
            act.wait_ge(stored, 32)

        @block.vector
        def _(dve):
            steps = [0]

            def link(ins):
                steps[0] += 1
                ins.then_inc(dve_step, 1)
                dve.wait_ge(dve_step, steps[0])

            v = nc.vector

            def split_lo(n, src, ring, width=PW):
                dve.wait_ge(hi_done, n + 1)
                out, h = lo[:, ring, 0:width], hi[:, ring, 0:width]
                if len(src.shape) == 3:
                    out, h = (a.rearrange("p (k c) -> p k c", k=src.shape[1]) for a in (out, h))
                elif len(src.shape) == 4:
                    out, h = (a.rearrange("p (k g c) -> p k g c", k=src.shape[1], g=src.shape[2]) for a in (out, h))
                v.tensor_tensor(out, src, h, ALU.subtract).then_inc(lo_done, 1)

            def mix_pieces(layer, a, b):
                for name, pieces, buf, _ in MIX_UNITS:
                    for q in range(pieces):
                        i = MIX_FIRST[name] + q
                        if a <= i < b:
                            src = (unit[buf][:, 4 * q:4 * q + 4, 0:256] if name == "kv"
                                   else unit[buf][:, 2 * q:2 * q + 2, :])
                            n = MIX_BASE[layer] + i
                            split_lo(n, src, n % RING)

            def norm_scale(n):
                dve.wait_ge(sumsq_done, 2 * (n + 1))
                v.tensor_scalar(ss[:, :], ss[:, :], 1.0 / D, EPS, ALU.mult, ALU.add).then_inc(ms_done, 1)
                dve.wait_ge(std_done, n + 1)
                link(v.reciprocal(rstd[:, :], std[:, :]))
                for t in range(NT):
                    ins = v.tensor_scalar(xn[:, t, :], x[:, t, :], rstd[:, t:t + 1], None, ALU.mult)
                ins.then_inc(xn_done, 1)

            def norm_lo(n, gain, banks):
                for k in range(KT):
                    dve.wait_ge(xThi_done, KT * n + 2 * (k // 2) + 2)
                    v.scalar_tensor_tensor(out=act_lo[:, k, :], in0=bank[banks[k // 2]][:, (k % 2) * 256:(k % 2) * 256 + 256],
                                           scalar=gain[:, k:k + 1], in1=act_hi[:, k, :],
                                           op0=ALU.mult, op1=ALU.subtract).then_inc(xTlo_done, 1)

            def rope_angles():
                dve.wait_ge(consts_in, 16 * CONSTS)
                dve.wait_ge(pool_done, POOL_STEPS)
                link(v.tensor_copy(pos_f[:, :], pos_i[:, :]))
                shape = [P, NT, HR]
                link(v.tensor_tensor(ang[:, :, :], pos_f[:, :].unsqueeze(2).to_broadcast(shape),
                                     inv_freq[:, :].unsqueeze(1).to_broadcast(shape), ALU.mult))
                big = 1.5 * 2.0 ** 23
                two_pi = 2 * np.pi
                c1 = 6.28125
                c2 = float(np.floor((two_pi - c1) * 2 ** 16) / 2 ** 16)
                c3 = two_pi - c1 - c2
                for f, quarter in ((0, 0.25), (1, 0.0)):
                    w = turns[:, f]
                    link(v.tensor_scalar(w, ang[:, :, :], 1.0 / two_pi, quarter, ALU.mult, ALU.add))
                    link(v.tensor_scalar(w, w, big, None, ALU.add))
                    link(v.tensor_scalar(w, w, big, None, ALU.subtract))
                    r = cs[:, f]
                    link(v.scalar_tensor_tensor(out=r, in0=w, scalar=-c1, in1=ang[:, :, :], op0=ALU.mult, op1=ALU.add))
                    link(v.scalar_tensor_tensor(out=r, in0=w, scalar=-c2, in1=r, op0=ALU.mult, op1=ALU.add))
                    link(v.scalar_tensor_tensor(out=r, in0=w, scalar=-c3, in1=r, op0=ALU.mult, op1=ALU.add))
                    if f == 0:
                        link(v.tensor_scalar(r, r, float(np.pi / 2), None, ALU.add))
                    ins = v.tensor_scalar(w, r, 3.1415925, -3.1415925, ALU.min, ALU.max)
                ins.then_inc(trig_arg, 1)

            def rope(layer):
                dve.wait_ge(qkv_out, 4 * (layer + 1))
                if layer == 0:
                    dve.wait_ge(trig_done, 1)
                heads = qkv[:, :, 0:AW + KVW].rearrange("p t (h d) -> p t h d", d=HD)
                x1, x2 = heads[:, :, :, 0:HR], heads[:, :, :, HR:ROT]
                shape = [P, NT, NH + NKV, HR]
                for t in range(NT):
                    cos = cs[:, 0, t].unsqueeze(1).to_broadcast([P, NH + NKV, HR])
                    sin = cs[:, 1, t].unsqueeze(1).to_broadcast([P, NH + NKV, HR])
                    for f, (a, b) in enumerate(((x1, cos), (x2, sin), (x2, cos), (x1, sin))):
                        ins = v.tensor_tensor(rope_t[:, f, t], a[:, t], b, ALU.mult)
                link(ins)
                v.tensor_tensor(x1, rope_t[:, 0], rope_t[:, 1], ALU.subtract)
                v.tensor_tensor(x2, rope_t[:, 2], rope_t[:, 3], ALU.add).then_inc(rope_done, 1)

            def masked_scores(layer, t):
                i = 2 * layer + t
                for b in range(4):
                    dve.wait_ge(scores_done, 4 * i + b + 1)
                    ins = v.scalar_tensor_tensor(
                        out=prob[:, b * 512:(b + 1) * 512].rearrange("p (h n) -> p h n", h=2),
                        in0=bank[b][:, :].rearrange("p (h n) -> p h n", h=2), scalar=HD ** -0.5,
                        in1=mask[:, t, :].unsqueeze(1).to_broadcast([P, 2, SEQ]), op0=ALU.mult, op1=ALU.add)
                link(ins)
                link(v.tensor_reduce(mx[:, :], prob.rearrange("p (h n) -> p h n", h=NH), AX, ALU.max))
                link(v.tensor_tensor(mx[:, :], mx[:, :], sink_sb[:, layer, :], ALU.max))
                v.tensor_scalar(nmx[:, t, :], mx[:, :], -1.0, None, ALU.mult)
                v.tensor_tensor(sinkd[:, t, :], sink_sb[:, layer, :], mx[:, :], ALU.subtract).then_inc(masked_done, 1)

            def denominators(layer, t):
                dve.wait_ge(exp_done, (NH + 1) * (2 * layer + t + 1))
                link(v.tensor_tensor(den[:, t, :], psums[:, t, :], esink[:, t, :], ALU.add))
                v.reciprocal(rden[:, t, :], den[:, t, :]).then_inc(rden_done, 1)

            def probT_copy(layer, t):
                dve.wait_ge(probT_done, 2 * layer + t + 1)
                for b in range(2, 4):
                    v.tensor_copy(probT[:, b * 512:(b + 1) * 512], bank[b][:, :]).then_inc(probT_out_v, 1)

            def attended(layer, t):
                dve.wait_ge(av_done, 2 * layer + t + 1)
                dve.wait_ge(rden_done, 2 * layer + t + 1)
                v.tensor_tensor(att[:, t, :].rearrange("p (h d) -> p h d", h=NH),
                                bank[6 + t][:, :].rearrange("p (h d) -> p h d", h=NH),
                                rden[:, t, :].unsqueeze(2).to_broadcast([P, NH, HD]), ALU.mult).then_inc(att_done, 1)

            def mixer(layer):
                base = MIX_BASE[layer]
                pieces = lambda a, b: mix_pieces(layer, a, b)
                if layer == 0:
                    rope_angles()
                else:
                    pieces(0, 4)
                    dve.wait_ge(lo_done, MIX_BASE[1])
                norm_scale(2 * layer)
                norm_lo(2 * layer, g_mix[:, layer, :], (0, 1, 2, 3))
                v.memset(zT[:, :, 0:1], 0.0)
                link(v.memset(zT[:, :, SEQ + 1:SEQ + 2], 0.0))
                pieces(4 if layer else 0, 12)
                rope(layer)
                pieces(12, 16)
                dve.wait_ge(qkT_done, layer + 1)
                v.tensor_copy(kT, bank[2][:, 0:SEQ]).then_inc(kT_out, 1)
                masked_scores(layer, 0)
                pieces(16, 18)
                dve.wait_ge(c_out, 2 * (layer + 1))
                dve.wait_ge(piece_used, base + MIX_FIRST["b"])
                for t in range(NT):
                    v.tensor_tensor(z[:, t, :], z[:, t, :], bank[6 + t][:, :], ALU.mult).then_inc(z_done, 1)
                denominators(layer, 0)
                probT_copy(layer, 0)
                pieces(18, 22)
                masked_scores(layer, 1)
                attended(layer, 0)
                pieces(22, 24)
                dve.wait_ge(zT_out, 2 * (layer + 1))
                for k in range(CT):
                    ins = v.tensor_scalar(yc[:, k, :], zT[:, k, 0:SEQ], cw[:, layer, 0, k:k + 1], None, ALU.mult)
                link(ins)
                for w in (1, 2):
                    for k in range(CT):
                        ins = v.scalar_tensor_tensor(out=yc[:, k, :], in0=zT[:, k, w:w + SEQ],
                                                     scalar=cw[:, layer, w, k:k + 1], in1=yc[:, k, :],
                                                     op0=ALU.mult, op1=ALU.add)
                    link(ins)
                dve.wait_ge(bT_done, layer + 1)
                for b in range(2):
                    c = slice(2 * b, 2 * b + 2)
                    ins = v.tensor_tensor(yc[:, c, :], yc[:, c, :], bank[4 + b][:, :].rearrange("p (c n) -> p c n", c=2),
                                          ALU.mult)
                ins.then_inc(yc_done, 1)
                probT_copy(layer, 1)
                denominators(layer, 1)
                attended(layer, 1)
                dve.wait_ge(attss_done, 2 * (layer + 1))
                v.tensor_scalar(ss_a[:, :], ss_a[:, :], 1.0 / AW, EPS, ALU.mult, ALU.add).then_inc(attms_done, 1)
                dve.wait_ge(cstd_done, layer + 1)
                link(v.reciprocal(rstd_c, std_c))
                v.tensor_tensor(yc, yc, rstd_c.unsqueeze(1).to_broadcast([P, CT, SEQ]), ALU.mult).then_inc(cn_done, 1)
                dve.wait_ge(attstd_done, layer + 1)
                link(v.reciprocal(rstd_a[:, :], std_a[:, :]))
                for t in range(NT):
                    ins = v.tensor_scalar(att[:, t, :], att[:, t, :], rstd_a[:, t:t + 1], None, ALU.mult)
                ins.then_inc(attn_done, 1)
                for i, k in enumerate((4, 5, 6, 7, 0, 1, 2, 3)):
                    dve.wait_ge(mixhi_done, 8 * layer + (i + 1 if k >= 4 else i // 2 * 2 + 2))
                    if k >= 4:
                        src, g = yc[:, k - 4, :], g_conv[:, layer, k - 4:k - 3]
                    else:
                        src, g = bank[k // 2][:, (k % 2) * 256:(k % 2) * 256 + 256], g_att[:, layer, k:k + 1]
                    v.scalar_tensor_tensor(out=act_lo[:, k, :], in0=src, scalar=g, in1=act_hi[:, k, :],
                                           op0=ALU.mult, op1=ALU.subtract).then_inc(mixlo_done, 1)
                pieces(24, 26)
                for c, name in enumerate(("out0", "out1")):
                    dve.wait_ge(piece_used, base + MIX_FIRST[name] + 4)
                    for t in range(NT):
                        xs = x[:, t, c * 512:(c + 1) * 512]
                        v.tensor_tensor(xs, xs, bank[4 + 2 * c + t][:, :], ALU.add).then_inc(x_changed, 1)

            def gu_src(s, half, q):
                return raw_gu[:, s, :, 2 * q:2 * q + 2, half * HALF:(half + 1) * HALF].rearrange("p g k c -> p k g c")

            def gu_pieces_lo(first, ring, slot, half):
                for q in range(4):
                    split_lo(first + q, gu_src(slot, half, q), (ring + q) % RING)

            def down_pieces_lo(first, ring, slot, half):
                for q in range(2):
                    split_lo(first + q, raw_dv[:, slot, 2 * half + q, :], (ring + q) % RING)

            def dense():
                b0 = DENSE_BASE

                def gate(h, half, wait_free=True):
                    dve.wait_ge(silu_done, h + 1)
                    for t in range(NT):
                        ins = v.tensor_tensor(gated[:, 2 * half + t, :], silu[:, t, :], bank[t][:, HALF:BLK], ALU.mult)
                    ins.then_inc(gated_done, 1)

                def turned(h):
                    dve.wait_ge(atTh_done, h + 1)
                    v.tensor_tensor(at_lo[:, :], bank[2][:, :], at_hi[:, :], ALU.subtract).then_inc(atTl_done, 1)

                for h in range(2):
                    gu_pieces_lo(b0 + 4 * h, b0 + 4 * h, 0, h)
                    gate(h, h)
                with dve.Fori(0, 2) as i:
                    for j in (1, 2):
                        for half in range(2):
                            h = 4 * i + 2 * j + half
                            ring = b0 + gu_first(2 * j + half)
                            first = dve.snap(24 * i + ring)
                            gu_pieces_lo(first, ring, j % 2, half)
                            turned(h - 2)
                            down_pieces_lo(first + 4, ring + 4, (j - 1) % 2, half)
                            gate(h, half)
                h = DH - 1
                first = b0 + gu_first(h)
                gu_pieces_lo(first, first, 1, 0)
                turned(h - 2)
                down_pieces_lo(first + 4, first + 4, 0, 0)
                gate(h, 0)
                turned(h - 1)
                down_pieces_lo(first + 6, first + 6, 0, 1)
                turned(h)
                down_pieces_lo(first + 8, first + 8, 1, 0)
                dve.wait_ge(piece_used, b0 + D_PIECES)
                for t in range(NT):
                    for c in range(2):
                        xs = x[:, t, c * 512:(c + 1) * 512]
                        v.tensor_tensor(xs, xs, bank[3 + 2 * t + c][:, :], ALU.add).then_inc(x_changed, 1)

            def route():
                dve.wait_ge(routhi_done, 1)
                v.tensor_tensor(rout_lo[:, :, :], rout[:, :, :], rout_hi[:, :, :], ALU.subtract).then_inc(routlo_done, 1)
                norm_lo(3, g_ffn[:, 1, :], (3, 4, 5, 6))
                dve.wait_ge(gain_in, 16)
                for t in range(NT):
                    v.tensor_tensor(xn[:, t, :], xn[:, t, :], gain_rows[:, :], ALU.mult).then_inc(xg_done, 1)
                dve.wait_ge(logits_done, 1)
                link(v.tensor_copy(logit[:, :, :], bank[2][:, 0:NT * NE].rearrange("p (t e) -> p t e", t=NT)))
                for t in range(NT):
                    ins = v.max(top[:, t, :], logit[:, t, :])
                link(ins)
                v.tensor_tensor(gdiff[:, :], top[:, :, 1], top[:, :, 0], ALU.subtract).then_inc(gdiff_done, 1)
                for t in range(NT):
                    ins = v.max_index(topi[:, t, :], top[:, t, :], logit[:, t, :])
                link(ins)
                link(v.tensor_copy(topf[:, :, :], topi[:, :, 0:2]))
                for c in range(2):
                    for t in range(NT):
                        ins = v.tensor_scalar(oneh[:, c, t, :], iota8[:, :], topf[:, t, c:c + 1], None, ALU.is_equal)
                link(ins)
                v.tensor_tensor(chosen[:, :, :], oneh[:, 0], oneh[:, 1], ALU.add).then_inc(chosen_done, 1)
                dve.wait_ge(gexp_done, 1)
                link(v.tensor_scalar(gden[:, :], gexp[:, :], 1.0, None, ALU.add))
                link(v.reciprocal(gates[:, :, 0], gden[:, :]))
                link(v.tensor_tensor(gates[:, :, 1], gates[:, :, 0], gexp[:, :], ALU.mult))
                for c in range(2):
                    for t in range(NT):
                        ins = v.tensor_scalar(gsum[:, c, t, :], oneh[:, c, t, :], gates[:, t, c:c + 1], None, ALU.mult)
                link(ins)
                by_expert = slot_of[:, 0:NE, :].rearrange("p e t -> p t e")
                gate_by_expert = gate_of[:, 0:NE, :].rearrange("p e t -> p t e")
                v.memset(slot_of[:, DUMMY:NCOL, :], -1.0)
                v.memset(gate_of[:, DUMMY:NCOL, :], 0.0)
                v.tensor_tensor(gate_by_expert, gsum[:, 0], gsum[:, 1], ALU.add)
                dve.wait_ge(rank_done, 1)
                ranks = bank[7][:, 0:NT * NE].rearrange("p (t e) -> p t e", t=NT)
                link(v.scalar_tensor_tensor(out=rank1[:, :, :], in0=ranks, scalar=1.0, in1=chosen[:, :, :],
                                            op0=ALU.add, op1=ALU.mult))
                link(v.tensor_scalar(by_expert, rank1[:, :, :], 1.0, None, ALU.subtract))
                counts = bank[7][:, NT * NE:NT * NE + NE]
                link(v.tensor_scalar(over[:, 0, :], counts, float(P) + 0.5, None, ALU.is_ge))
                src = 0
                for i, shift in enumerate((1, 2, 4)):
                    v.tensor_copy(over[:, i + 1, 0:shift], over[:, src, 0:shift])
                    link(v.tensor_tensor(over[:, i + 1, shift:NE], over[:, src, shift:NE],
                                         over[:, src, 0:NE - shift], ALU.add))
                    src = i + 1
                for i in range(XP):
                    ins = v.scalar_tensor_tensor(out=xsel[:, i, :], in0=over[:, 3, :], scalar=float(i + 1),
                                                 in1=over[:, 0, :], op0=ALU.is_equal, op1=ALU.mult)
                link(ins)
                shape = [P, XP, NE]
                link(v.tensor_tensor(xid[:, :, :], xsel[:, :, :], iota8[:, :].unsqueeze(1).to_broadcast(shape), ALU.mult))
                v.tensor_reduce(plan_f[:, 0:XP], xid[:, :, :], AX, ALU.add)
                for t in range(NT):
                    ins = v.tensor_tensor(xprod[:, :, t, :], xsel[:, :, :],
                                          rank1[:, t, :].unsqueeze(1).to_broadcast(shape), ALU.mult)
                link(ins)
                link(v.tensor_reduce(slot_of[:, NE:DUMMY, :], xprod[:, :, :, :], AX, ALU.add))
                link(v.tensor_scalar(slot_of[:, NE:DUMMY, :], slot_of[:, NE:DUMMY, :], float(P) + 1.0, None, ALU.subtract))
                for t in range(NT):
                    ins = v.tensor_tensor(xprod[:, :, t, :], xsel[:, :, :],
                                          gate_of[:, 0:NE, t].unsqueeze(1).to_broadcast(shape), ALU.mult)
                link(ins)
                link(v.tensor_reduce(gate_of[:, NE:DUMMY, :], xprod[:, :, :, :], AX, ALU.add))
                v.tensor_scalar(plan_t[:, 0:1], over[:, 3, NE - 1:NE], 0.5, None, ALU.is_ge)
                link(v.tensor_scalar(plan_t[:, 1:2], over[:, 3, NE - 1:NE], 2.5, None, ALU.is_ge))
                link(v.tensor_tensor(plan_f[:, 5:6], plan_t[:, 0:1], plan_t[:, 1:2], ALU.add))
                link(v.tensor_scalar(plan_f[:, 4:5], plan_f[:, 5:6], 2.0, float(NE), ALU.mult, ALU.add))
                v.tensor_copy(plan[:, 0:6], plan_f[:, 0:6]).then_inc(plan_done, 1)

            def build_sel(p):
                for t in range(NT):
                    ins = v.tensor_scalar(sel[:, t, :], iota[:, :], slot_of[:, p, t:t + 1], None, ALU.is_equal)
                ins.then_inc(sel_done, 1)

            def build_gsel(p):
                for t in range(NT):
                    ins = v.tensor_scalar(gsel[:, t, :], iota[:, :], slot_of[:, p, t:t + 1],
                                          gate_of[:, p, t:t + 1], ALU.is_equal, ALU.mult)
                ins.then_inc(gsel_done, 1)

            def experts():
                b0 = MOE_BASE

                def gate(half, n):
                    dve.wait_ge(silu_done, n + 1)
                    v.tensor_tensor(gated[:, half, :], silu[:, half, :], bank[half][:, HALF:BLK], ALU.mult)\
                        .then_inc(gated_done, 1)

                def turned(half, n):
                    dve.wait_ge(atTh_done, n + 1)
                    c = slice(half * 256, half * 256 + 256)
                    v.tensor_tensor(at_lo[:, c], bank[2][:, c], at_hi[:, c], ALU.subtract).then_inc(atTl_done, 1)

                def gather_lo(p):
                    for b in range(2):
                        dve.wait_ge(xehi_done, 2 * p + b + 1)
                        v.tensor_tensor(act_lo[:, 4 * b:4 * b + 4, 0:P],
                                        bank[5 + b][:, :].rearrange("p (k n) -> p k n", k=4),
                                        act_hi[:, 4 * b:4 * b + 4, 0:P], ALU.subtract).then_inc(xelo_done, 1)

                def rows_out(p):
                    dve.wait_ge(scattered, 4 * p + 1)
                    dve.wait_ge(piece_used, b0 + E_PIECES * p)
                    v.tensor_copy(y[:, 512:D], bank[4][:, :]).then_inc(y_dve, 1)

                def add_rows(p):
                    dve.wait_ge(x_changed, 12 + 4 * p)
                    for r, b in enumerate((5, 6, 7, 5)):
                        t, c = r // 2, r % 2
                        dve.wait_ge(scattered, 4 * p + r + 2)
                        xs = x[:, t, c * 512:(c + 1) * 512]
                        v.tensor_tensor(xs, xs, bank[b][:, :], ALU.add).then_inc(x_changed, 1)

                build_sel(0)
                build_gsel(0)
                dve.wait_ge(plan_done, 1)
                passes = dve.value_load(plan[0:1, 4:5], min_val=NE, max_val=NE + XP)
                gather_lo(0)
                with dve.Fori(0, passes) as p:
                    first = dve.snap(b0 + E_PIECES * p)
                    n0 = dve.snap(DH + EH * p)
                    s0 = dve.snap(p % 2)
                    gu_pieces_lo(first, b0, s0, 0)
                    rows_out(p)
                    for q in range(2):
                        split_lo(first + 4 + q, gu_src(s0, 1, q), (b0 + 4 + q) % RING)
                    add_rows(p)
                    for q in range(2, 4):
                        split_lo(first + 4 + q, gu_src(s0, 1, q), (b0 + 4 + q) % RING)
                    gate(0, n0)
                    dve.wait_ge(gathered, p + 1)
                    build_sel(p + 1)
                    with dve.Fori(1, EB) as j:
                        f = dve.snap(first + 12 * j - 4)
                        n = dve.snap(n0 + 2 * j)
                        s = dve.snap((p + j) % 2)
                        s1 = dve.snap((p + j + 1) % 2)
                        gu_pieces_lo(f, b0 + 8, s, 0)
                        turned(0, n - 2)
                        gate(1, n - 1)
                        down_pieces_lo(f + 4, b0 + 12, s1, 0)
                        gu_pieces_lo(f + 6, b0 + 14, s, 1)
                        turned(1, n - 1)
                        gate(0, n)
                        down_pieces_lo(f + 10, b0 + 18, s1, 1)
                    f = dve.snap(first + d_first(EH - 2, EH))
                    n = dve.snap(n0 + EH)
                    turned(0, n - 2)
                    gate(1, n - 1)
                    down_pieces_lo(f, b0 + 8, s0, 0)
                    gather_lo(p + 1)
                    turned(1, n - 1)
                    down_pieces_lo(f + 2, b0 + 10, s0, 1)
                    dve.wait_ge(gselT_done, p + 1)
                    build_gsel(p + 1)
                rows_out(passes)
                add_rows(passes)
                return passes

            mixer(0)
            norm_scale(1)
            norm_lo(1, g_ffn[:, 0, :], (3, 4, 5, 6))
            dense()
            mixer(1)
            norm_scale(3)
            route()
            experts()
            dve.wait_ge(sumsq_done, 10)
            v.tensor_scalar(ss[:, :], ss[:, :], 1.0 / D, EPS, ALU.mult, ALU.add).then_inc(ms_done, 1)
            dve.wait_ge(std_done, 5)
            dve.wait_ge(gain_in, 32)
            link(v.reciprocal(rstd[:, :], std[:, :]))
            for t in range(NT):
                v.scalar_tensor_tensor(out=xn[:, t, :], in0=x[:, t, :], scalar=rstd[:, t:t + 1],
                                       in1=gain_rows[:, :], op0=ALU.mult, op1=ALU.mult).then_inc(final_done, 1)

        @block.tensor
        def _(pe):
            mm, tr = nc.tensor.matmul, nc.tensor.transpose

            def transposed_norm(n, banks):
                pe.wait_ge(xn_done, n + 1)
                for b in range(4):
                    for k in (2 * b, 2 * b + 1):
                        for t in range(NT):
                            c = (k % 2) * 256 + t * P
                            ins = tr(bank[banks[b]][:, c:c + P], xn[:, t, k:D:KT], ident[:, :])
                    ins.then_inc(xT_done, 1)

            def three(out, ah, al, wh, wl, start, stop, **kw):
                mm(out, ah, wh, start=start, stop=False, **kw)
                mm(out, ah, wl, start=False, stop=False, **kw)
                return mm(out, al, wh, start=False, stop=stop, **kw)

            def mix_pieces(layer, name, banks, q0, q1):
                wide, kk = (256, 4) if name == "kv" else (512, 2)
                for q in range(q0, q1):
                    n = MIX_BASE[layer] + MIX_FIRST[name] + q
                    r = n % RING
                    pe.wait_ge(lo_done, n + 1)
                    for i in range(kk):
                        k = kk * q + i
                        if name == "q":
                            pe.wait_ge(xTlo_done, 2 * KT * layer + k + 1)
                        c = slice(i * wide, (i + 1) * wide)
                        for t in range(NT):
                            tt = slice(t * P, (t + 1) * P)
                            ins = three(bank[banks[t]][:, 0:wide], act_hi[:, k, tt], act_lo[:, k, tt],
                                        hi[:, r, c], lo[:, r, c], k == 0, k == KT - 1)
                    ins.then_inc(piece_used, 1)

            def scores(layer, t):
                for b in range(4):
                    for i in range(2):
                        h = 2 * b + i
                        rows = slice(HD * (h // 4), HD * (h // 4) + HD)
                        ins = mm(bank[b][:, i * SEQ:(i + 1) * SEQ], qT[rows, h % 4, t * P:(t + 1) * P],
                                 kT[rows, :], start=True, stop=True)
                    ins.then_inc(scores_done, 1)

            def turn_probs(layer, t):
                pe.wait_ge(exp_done, (NH + 1) * (2 * layer + t + 1))
                for h in range(NH):
                    for kt in range(NT):
                        c = (h % 2) * 256 + kt * P
                        ins = tr(bank[h // 2][:, c:c + P], prob[:, h * 256 + kt * P:h * 256 + kt * P + P], ident[:, :])
                ins.then_inc(probT_done, 1)

            def values(layer, t):
                i = 2 * (2 * layer + t + 1)
                pe.wait_ge(probT_out_a, i)
                pe.wait_ge(probT_out_v, i)
                for h in range(NH):
                    g = AW + KVW + HD * (h // (NH // NKV))
                    for kt in range(NT):
                        ins = mm(bank[6 + t][:, h * HD:(h + 1) * HD], probT[:, h * 256 + kt * P:h * 256 + kt * P + P],
                                 qkv[:, kt, g:g + HD], start=kt == 0, stop=kt == 1)
                ins.then_inc(av_done, 1)

            def mixer(layer):
                if layer == 0:
                    pe.wait_ge(pool_done, POOL_STEPS)
                transposed_norm(2 * layer, (0, 1, 2, 3))
                mix_pieces(layer, "q", (4, 5), 0, 4)
                mix_pieces(layer, "kv", (6, 7), 0, 2)
                pe.wait_ge(qkv_out, 4 * layer + 2)
                mix_pieces(layer, "c", (4, 5), 0, 4)
                pe.wait_ge(rope_done, layer + 1)
                for c in range(4):
                    for t in range(NT):
                        ins = tr(bank[c // 2][:, (c % 2) * 256 + t * P:(c % 2) * 256 + t * P + P],
                                 qkv[:, t, c * P:(c + 1) * P], ident[:, :])
                for t in range(NT):
                    ins = tr(bank[2][:, t * P:(t + 1) * P], qkv[:, t, AW:AW + KVW], ident[:, :])
                ins.then_inc(qkT_done, 1)
                pe.wait_ge(qT_out, 2 * (layer + 1))
                pe.wait_ge(kT_out, layer + 1)
                scores(layer, 0)
                pe.wait_ge(qkv_out, 4 * layer + 4)
                mix_pieces(layer, "u", (6, 7), 0, 4)
                turn_probs(layer, 0)
                pe.wait_ge(c_out, 2 * (layer + 1))
                mix_pieces(layer, "b", (4, 5), 0, 2)
                pe.wait_ge(probT_out_a, 2 * (2 * layer + 1))
                pe.wait_ge(probT_out_v, 2 * (2 * layer + 1))
                scores(layer, 1)
                pe.wait_ge(z_done, 2 * (layer + 1))
                values(layer, 0)
                mix_pieces(layer, "b", (4, 5), 2, 4)
                pe.wait_ge(b_out, 2 * (layer + 1))
                for src, signal in ((z, zT_done), (bb, bT_done)):
                    if signal is bT_done:
                        pe.wait_ge(zT_out, 2 * (layer + 1))
                    for k in range(CT):
                        for t in range(NT):
                            c = (k % 2) * 256 + t * P
                            ins = tr(bank[4 + k // 2][:, c:c + P], src[:, t, k:CW:CT], ident[:, :])
                    ins.then_inc(signal, 1)
                turn_probs(layer, 1)
                values(layer, 1)
                pe.wait_ge(sq_done, layer + 1)
                for k in range(CT):
                    ins = mm(bank[2][:, 0:SEQ], ones[:, :], sq[:, k, :], start=k == 0, stop=k == CT - 1)
                ins.then_inc(cms_done, 1)
                pe.wait_ge(attn_done, layer + 1)
                for k in range(4):
                    for t in range(NT):
                        c = (k % 2) * 256 + t * P
                        ins = tr(bank[k // 2][:, c:c + P], att[:, t, k:AW:4], ident[:, :])
                ins.then_inc(attT_done, 1)
                pe.wait_ge(mixlo_done, 8 * (layer + 1))
                mix_pieces(layer, "out0", (4, 5), 0, 4)
                mix_pieces(layer, "out1", (6, 7), 0, 4)

            def gu_pieces(first, ring, tiles):
                for q in range(4):
                    pe.wait_ge(lo_done, first + q + 1)
                    r = (ring + q) % RING
                    for i in range(2):
                        k = 2 * q + i
                        c = slice(i * BLK, (i + 1) * BLK)
                        for b, tt in tiles:
                            ins = three(bank[b][:, :], act_hi[:, k, tt], act_lo[:, k, tt], hi[:, r, c], lo[:, r, c],
                                        k == 0, k == KT - 1)
                    ins.then_inc(piece_used, 1)

            def down_pieces(first, ring, tiles, last=False):
                for q in range(2):
                    pe.wait_ge(lo_done, first + q + 1)
                    r = (ring + q) % RING
                    for b, col, step in tiles:
                        tt = slice(col + q * step, col + q * step + P)
                        for c in range(2):
                            cc = slice(c * 512, (c + 1) * 512)
                            ins = three(bank[b + c][:, :], at_hi[:, tt], at_lo[:, tt], hi[:, r, cc], lo[:, r, cc],
                                        False, last and q == 1, skip_group_check=True)
                    ins.then_inc(piece_used, 1)

            def clear(banks):
                for b in banks:
                    ins = mm(bank[b][:, :], zeros[:, 0:P], zeros[:, :], start=True, stop=True)
                return ins

            def dense():
                b0 = DENSE_BASE
                tiles = [(t, slice(t * P, (t + 1) * P)) for t in range(NT)]
                outs = [(3 + 2 * t, t * P, NT * P) for t in range(NT)]

                def gu(h, first, ring):
                    if not isinstance(h, int) or h > 0:
                        pe.wait_ge(gated_done, h)
                    gu_pieces(first, ring, tiles)

                def turn(h, half):
                    pe.wait_ge(gated_done, h + 1)
                    if not isinstance(h, int) or h > 0:
                        pe.wait_ge(atTl_done, h)
                    for i in range(2):
                        for t in range(NT):
                            c = i * NT * P + t * P
                            ins = tr(bank[2][:, c:c + P], gated[:, 2 * half + t, i * P:(i + 1) * P], ident[:, :])
                    ins.then_inc(gT_done, 1)

                def down(h, first, ring, last=False):
                    pe.wait_ge(atTl_done, h + 1)
                    down_pieces(first, ring, outs, last)

                pe.wait_ge(xTlo_done, 2 * KT)
                clear((3, 4, 5, 6))
                gu(0, b0, b0)
                gu(1, b0 + 4, b0 + 4)
                turn(0, 0)
                with pe.Fori(0, 2) as i:
                    for j in (1, 2):
                        for half in range(2):
                            h = 4 * i + 2 * j + half
                            ring = b0 + gu_first(2 * j + half)
                            first = pe.snap(24 * i + ring)
                            gu(h, first, ring)
                            down(h - 2, first + 4, ring + 4)
                            turn(h - 1, 1 - half)
                h = DH - 1
                first = b0 + gu_first(h)
                gu(h, first, first)
                down(h - 2, first + 4, first + 4)
                turn(h - 1, 1)
                down(h - 1, first + 6, first + 6)
                turn(h, 0)
                down(h, first + 8, first + 8, last=True)

            def route():
                pe.wait_ge(routlo_done, 1)
                pe.wait_ge(xTlo_done, 4 * KT)
                for t in range(NT):
                    tt = slice(t * P, (t + 1) * P)
                    for k in range(KT):
                        ins = three(bank[2][:, t * NE:(t + 1) * NE], act_hi[:, k, tt], act_lo[:, k, tt],
                                    rout_hi[:, k, :], rout_lo[:, k, :], k == 0, k == KT - 1)
                ins.then_inc(logits_done, 1)
                pe.wait_ge(chosen_done, 1)
                r = bank[7]
                mm(r[:, 0:NE], before[:, :], chosen[:, 0, :], start=True, stop=True)
                mm(r[:, NE:2 * NE], ones[:, :], chosen[:, 0, :], start=True, stop=False)
                mm(r[:, NE:2 * NE], before[:, :], chosen[:, 1, :], start=False, stop=True)
                mm(r[:, 2 * NE:3 * NE], ones[:, :], chosen[:, 0, :], start=True, stop=False)
                mm(r[:, 2 * NE:3 * NE], ones[:, :], chosen[:, 1, :], start=False, stop=True).then_inc(rank_done, 1)

            def experts():
                b0 = MOE_BASE

                def gu(half, first, ring, n):
                    pe.wait_ge(gated_done, n - 1)
                    gu_pieces(first, ring, [(half, slice(0, P))])

                def turn(half, n):
                    pe.wait_ge(gated_done, n + 1)
                    pe.wait_ge(atTl_done, n)
                    for i in range(2):
                        c = half * 256 + i * P
                        ins = tr(bank[2][:, c:c + P], gated[:, half, i * P:(i + 1) * P], ident[:, :])
                    ins.then_inc(gT_done, 1)

                def down(half, first, ring, n, last=False):
                    pe.wait_ge(atTl_done, n + 1)
                    down_pieces(first, ring, [(3, half * 256, P)], last)

                def gather(p):
                    pe.wait_ge(sel_done, p + 1)
                    for k in range(KT):
                        for t in range(NT):
                            ins = mm(bank[5 + k // 4][:, (k % 4) * P:(k % 4 + 1) * P], xn[:, t, k:D:KT], sel[:, t, :],
                                     start=t == 0, stop=t == 1)
                    ins.then_inc(gathered, 1)

                def scatter(p):
                    pe.wait_ge(y_act, p + 1)
                    pe.wait_ge(y_dve, p + 1)
                    pe.wait_ge(gselT_out, p + 1)
                    for r, b in enumerate((5, 6, 7, 5)):
                        t, c = r // 2, r % 2
                        if r == 3:
                            pe.wait_ge(x_changed, 12 + 4 * p + 1)
                        mm(bank[b][:, :], gselT[:, t * P:(t + 1) * P], y[:, c * 512:(c + 1) * 512],
                           start=True, stop=True).then_inc(scattered, 1)

                pe.wait_ge(plan_done, 1)
                passes = pe.value_load(plan[0:1, 4:5], min_val=NE, max_val=NE + XP)
                pe.wait_ge(xg_done, 2)
                clear((3, 4)).then_inc(scattered, 1)
                gather(0)
                with pe.Fori(0, passes) as p:
                    first = pe.snap(b0 + E_PIECES * p)
                    n0 = pe.snap(DH + EH * p)
                    pe.wait_ge(xelo_done, 2 * p + 2)
                    gu(0, first, b0, n0)
                    scatter(p)
                    clear((3, 4))
                    gu(1, first + 4, b0 + 4, n0 + 1)
                    turn(0, n0)
                    with pe.Fori(1, EB) as j:
                        f = pe.snap(first + 12 * j - 4)
                        n = pe.snap(n0 + 2 * j)
                        gu(0, f, b0 + 8, n)
                        down(0, f + 4, b0 + 12, n - 2)
                        turn(1, n - 1)
                        gu(1, f + 6, b0 + 14, n + 1)
                        down(1, f + 10, b0 + 18, n - 1)
                        turn(0, n)
                    f = pe.snap(first + d_first(EH - 2, EH))
                    n = pe.snap(n0 + EH)
                    pe.wait_ge(x_changed, 12 + 4 * (p + 1))
                    gather(p + 1)
                    pe.wait_ge(gsel_done, p + 1)
                    for t in range(NT):
                        ins = tr(bank[7][:, t * P:(t + 1) * P], gsel[:, t, :], ident[:, :])
                    ins.then_inc(gselT_done, 1)
                    turn(1, n - 1)
                    down(0, f, b0 + 8, n - 2)
                    down(1, f + 2, b0 + 10, n - 1, last=True)
                scatter(passes)

            mixer(0)
            transposed_norm(1, (3, 4, 5, 6))
            dense()
            mixer(1)
            transposed_norm(3, (3, 4, 5, 6))
            route()
            experts()


_INS = ["x", "positions", "mix_norm_g", "w_in", "conv_w", "sink", "att_out_g", "conv_out_g", "w_out",
        "ffn_norm_g", "dense_w_gate", "dense_w_up", "dense_w_down", "router_w",
        "moe_w_gate", "moe_w_up", "moe_w_down", "final_norm_g"]


def kernel(**inputs):
    import concourse.bacc as bacc
    from concourse.bass_utils import run_bass_kernel_spmd

    nc = bacc.Bacc("TRN2", target_bir_lowering=False, num_devices=1)
    arrays, args = {}, []
    for name in _INS:
        a = np.ascontiguousarray(inputs[name])
        arrays[f"in_{name}"] = a
        args.append(nc.dram_tensor(f"in_{name}", a.shape, mybir.dt.from_np(a.dtype), kind="ExternalInput").ap())
    out = nc.dram_tensor("out", (1, SEQ, D), F32, kind="ExternalOutput").ap()
    build_trunk(nc, *args, out)
    return run_bass_kernel_spmd(nc, [arrays], core_ids=[0]).results[0]["out"]
```

```python
from contextlib import ExitStack

import numpy as np

import concourse.bass as bass
from concourse import mybir

ALU = mybir.AluOpType
ACT = mybir.ActivationFunctionType
AX = mybir.AxisListType.X
F32 = mybir.dt.float32
F32R = mybir.dt.float32r
I32 = mybir.dt.int32
U32 = mybir.dt.uint32

P = 128
D = 1024
KT = D // P
SEQ = 256
NT = SEQ // P
NH, NKV, HD = 8, 2, 64
AW = NH * HD
KVW = NKV * HD
CW = D - AW
CT = CW // P
QKV = AW + 2 * KVW
ROT = HD // 4
HR = ROT // 2
WINDOW = 128
THETA = 500000.0
EPS = 1e-5
NEG = -1e30
FD = 2816
NE = 8
FE = 3584
HALF = 256
BLK = 2 * HALF
RING = 6
PW = 1024
NCOL = NE + 1

MIX_UNITS = [("q", 4, 0, 1), ("kv", 2, 1, 1), ("c", 4, 2, 1), ("u", 4, 3, 1), ("b", 4, 0, 1),
             ("out0", 4, 1, 2), ("out1", 4, 2, 2)]
MIX_FIRST = {}
MIX_PIECES = 0
for _n, _p, _, _ in MIX_UNITS:
    MIX_FIRST[_n] = MIX_PIECES
    MIX_PIECES += _p


def gu_first(h):
    return 4 * h if h < 2 else 8 + 6 * (h - 2)


def d_first(h, halves):
    return 8 + 6 * h + 4 if h < halves - 2 else 8 + 6 * (halves - 2) + 2 * (h - halves + 2)


DH = FD // HALF
EH = FE // HALF
EB = EH // 2
D_PIECES = 6 * DH
E_PIECES = 6 * EH
MIX_BASE = [0, MIX_PIECES + D_PIECES]
DENSE_BASE = MIX_PIECES
MOE_BASE = MIX_BASE[1] + MIX_PIECES
assert E_PIECES % RING == 0


CONSTS = 7
POOL_STEPS = 6 + NE + 4


def build_trunk(nc, x_d, pos_d, mix_g, w_in, conv_w, sink, att_g, conv_g, w_out, ffn_g, dg, du, dd,
                router, eg, eu, ed, final_g, out_d):
    ctx = ExitStack()
    with ctx:
        def sb(name, shape, dt=F32):
            return ctx.enter_context(nc.sbuf_tensor(name, shape, dt))

        def sem(name):
            return ctx.enter_context(nc.semaphore(name))

        bank = [ctx.enter_context(nc.psum_tensor(f"bank{i}", [P, 512], F32)) for i in range(8)]

        raw_gu = sb("raw_gu", [P, 2, 2, KT, BLK])
        raw_d = sb("raw_d", [P, 2, 8192 // 2])
        hi = sb("hi", [P, RING, PW], F32R)
        lo = sb("lo", [P, RING, PW], F32R)
        x = sb("x", [P, NT, D])
        xn = sb("xn", [P, NT, D])
        act_hi = sb("act_hi", [P, KT, SEQ], F32R)
        act_lo = sb("act_lo", [P, KT, SEQ], F32R)
        at_hi = sb("at_hi", [P, 512], F32R)
        at_lo = sb("at_lo", [P, 512], F32R)
        gated = sb("gated", [P, 4, HALF])
        silu = sb("silu", [P, 2, HALF])
        y = sb("y", [P, D])
        gain_rows = sb("gain_rows", [P, D])
        sel = sb("sel", [P, NT, P])
        logT = sel[0:2 * NE, :, :].rearrange("e t n -> e (t n)")
        gsel = sb("gsel", [P, NT, P])
        gselT = sb("gselT", [P, SEQ])
        zeros = sb("zeros", [P, 512], F32R)
        mask = sb("mask", [P, NT, SEQ])
        ident = sb("ident", [P, P])
        ones = sb("ones", [P, P])
        before = sb("before", [P, P])
        gsel2 = sb("gsel2", [P, NT, P])
        iota = sb("iota", [P, SEQ])
        four_to = sb("four_to", [P, NE])
        inv_freq = sb("inv_freq", [P, HR])
        pos_i = sb("pos_i", [P, NT], I32)
        pos_f = sb("pos_f", [P, NT])
        ang = sb("ang", [P, NT, HR])
        turns = sb("turns", [P, 2, NT, HR])
        cs = sb("cs", [P, 2, NT, HR])
        eps = sb("eps", [P, 1])
        table_warm = sb("table_warm", [P, 1])
        g_mix = sb("g_mix", [P, 2, KT])
        g_ffn = sb("g_ffn", [P, 2, KT])
        g_att = sb("g_att", [P, 2, 4])
        g_conv = sb("g_conv", [P, 2, CT])
        cw = sb("cw", [P, 2, 3, CT])
        sink_sb = sb("sink_sb", [P, 2, NH])
        rout = sb("rout", [P, KT, NE])
        rout_hl = sb("rout_hl", [P, KT, 2 * NE], F32R)
        ss = sb("ss", [P, NT])
        ss_part = sb("ss_part", [P, NT, 2])
        std = sb("std", [P, NT])
        rstd = sb("rstd", [P, NT])
        ss_a = sb("ss_a", [P, NT])
        std_a = sb("std_a", [P, NT])
        rstd_a = sb("rstd_a", [P, NT])
        mx = sb("mx", [P, NH])
        nmx = sb("nmx", [P, NT, NH])
        sinkd = sb("sinkd", [P, NT, NH])
        psums = sb("psums", [P, NT, NH])
        esink = sb("esink", [P, NT, NH])
        den = sb("den", [P, NT, NH])
        rden = sb("rden", [P, NT, NH])
        logit = sb("logit", [P, NT, NE])
        top = sb("top", [P, NT, 8])
        topi = sb("topi", [P, NT, 8], U32)
        topf = sb("topf", [P, NT, 2])
        gdiff = sb("gdiff", [P, NT])
        gexp = sb("gexp", [P, NT])
        gden = sb("gden", [P, NT])
        gates = sb("gates", [P, NT, 2])
        oneh = sb("oneh", [P, 2, NT, NE])
        chosen = sb("chosen", [P, NT, NE])
        gsum = sb("gsum", [P, 2, NT, NE])
        rank1 = sb("rank1", [P, NT, NE])
        slot_of = sb("slot_of", [P, NCOL, NT])
        gate_of = sb("gate_of", [P, NCOL, NT])
        over = sb("over", [P, 4, NE])
        two = sb("two", [P, NE])
        plan_f = sb("plan_f", [P, 1])
        plan = sb("plan", [P, 1], I32)

        unit = [raw_gu[:, n // 2, n % 2] for n in range(4)]
        mixbuf = raw_d[:, :, :].rearrange("p a b -> p (a b)")
        prob = mixbuf[:, 0:2048]
        probT = mixbuf[:, 2048:4096]
        rope_t = mixbuf[:, 2048:2048 + 4 * NT * 10 * HR].rearrange("p (f t h j) -> p f t h j", f=4, t=NT, h=10)
        qkv = mixbuf[:, 4096:4096 + NT * QKV].rearrange("p (t n) -> p t n", t=NT)
        qT = mixbuf[:, 5632:6656].rearrange("p (c n) -> p c n", c=4)
        kT = mixbuf[:, 6656:6912]
        zT = mixbuf[:, 6912:6912 + CT * (SEQ + 2)].rearrange("p (c n) -> p c n", c=CT)
        att = qT.rearrange("p c n -> p (c n)").rearrange("p (t n) -> p t n", t=NT)
        z = xn[:, :, 0:CW]
        bb = xn[:, :, CW:D]
        yc = y[:, :].rearrange("p (c n) -> p c n", c=CT)
        sq = gated[:, :, :]
        rstd_c = silu[:, 0, :]
        std_c = silu[:, 1, :]

        unit_in = [sem(f"unit_in{n}") for n in range(4)]
        down_in = [sem(f"down_in{n}") for n in range(2)]
        hi_done, lo_done, piece_used = sem("hi_done"), sem("lo_done"), sem("piece_used")
        x_in = [sem("x_in0"), sem("x_in1")]
        consts_in = sem("consts_in")
        gain_in = sem("gain_in")
        stored = sem("stored")
        pool_done = sem("pool_done")
        dve_step, act_step = sem("dve_step"), sem("act_step")
        trig_arg = sem("trig_arg")
        trig_done = sem("trig_done")
        x_changed = sem("x_changed")
        sumsq_done, ms_done, std_done, xn_done = sem("sumsq_done"), sem("ms_done"), sem("std_done"), sem("xn_done")
        xT_done, xThi_done, xTlo_done = sem("xT_done"), sem("xThi_done"), sem("xTlo_done")
        qkv_out, rope_done = sem("qkv_out"), sem("rope_done")
        qkT_done, qT_out, kT_out = sem("qkT_done"), sem("qT_out"), sem("kT_out")
        scores_done, masked_done, exp_done, rden_done = sem("scores_done"), sem("masked_done"), sem("exp_done"), sem("rden_done")
        probT_done, probT_out_a, probT_out_v = sem("probT_done"), sem("probT_out_a"), sem("probT_out_v")
        av_done, att_done, attss_done, attms_done, attstd_done, attn_done = (
            sem("av_done"), sem("att_done"), sem("attss_done"), sem("attms_done"), sem("attstd_done"), sem("attn_done"))
        c_out, z_done, b_out, zT_done, zT_out, bT_done, yc_done, sq_done, cms_done, cstd_done, cn_done = (
            sem("c_out"), sem("z_done"), sem("b_out"), sem("zT_done"), sem("zT_out"), sem("bT_done"),
            sem("yc_done"), sem("sq_done"), sem("cms_done"), sem("cstd_done"), sem("cn_done"))
        attT_done, mixhi_done, mixlo_done = sem("attT_done"), sem("mixhi_done"), sem("mixlo_done")
        silu_done, gated_done, gT_done, atTh_done, atTl_done = (
            sem("silu_done"), sem("gated_done"), sem("gT_done"), sem("atTh_done"), sem("atTl_done"))
        routhi_done, routlo_done = sem("routhi_done"), sem("routlo_done")
        logits_done, gdiff_done, gexp_done, chosen_done, rank_done = (
            sem("logits_done"), sem("gdiff_done"), sem("gexp_done"), sem("chosen_done"), sem("rank_done"))
        plan_done = sem("plan_done")
        logT_done, logT_out = sem("logT_done"), sem("logT_out")
        sel_done, gsel_done, gathered, xehi_done, xelo_done = (
            sem("sel_done"), sem("gsel_done"), sem("gathered"), sem("xehi_done"), sem("xelo_done"))
        gselT_done, gselT_out = sem("gselT_done"), sem("gselT_out")
        y_act, y_dve, scattered = sem("y_act"), sem("y_dve"), sem("scattered")
        sel2_done, gathered2, xehi2_done, xelo2_done = (
            sem("sel2_done"), sem("gathered2"), sem("xehi2_done"), sem("xelo2_done"))
        gsel2_done, gselT2_done, gselT2_out = sem("gsel2_done"), sem("gselT2_done"), sem("gselT2_out")
        y2_act, y2_dve, scattered2, x_changed2 = sem("y2_act"), sem("y2_dve"), sem("scattered2"), sem("x_changed2")
        final_done, xg_done = sem("final_done"), sem("xg_done")
        ident_done, gain0_in, pos_in = sem("ident_done"), sem("gain0_in"), sem("pos_in")


        unit_seen = [[0] * 4]
        mix_landed = []
        for layer in range(2):
            seen, landed = list(unit_seen[-1]), {}
            for name, _, buf, loads in MIX_UNITS:
                seen[buf] += 16 * loads
                landed[name] = (buf, seen[buf])
            mix_landed.append(landed)
            unit_seen.append(seen)
            if layer == 0:
                unit_seen.append([n + 16 * 3 for n in seen])
        dense_seen, moe_seen = unit_seen[1], unit_seen[3]

        DOWN0 = 3 * 16

        block = ctx.enter_context(nc.Block())

        w_in_v = w_in.rearrange("l (p k) n -> l p k n", k=KT)
        w_out_v = w_out.rearrange("l (h p k) n -> l h p k n", h=2, k=4)
        dg_v = dg.rearrange("l (p k) n -> l p k n", k=KT)
        du_v = du.rearrange("l (p k) n -> l p k n", k=KT)
        dd_v = dd.rearrange("l (t p) n -> l p t n", p=P)
        eg_v = eg.rearrange("l e (p k) n -> (l e) p k n", k=KT)
        eu_v = eu.rearrange("l e (p k) n -> (l e) p k n", k=KT)
        ed_v = ed.rearrange("l e (t p) n -> (l e) p t n", p=P)
        raw_dv = raw_d[:, :, :].rearrange("p s (t n) -> p s t n", t=4)

        @block.sync
        def _(sp):
            for t in range(NT):
                sp.dma_start(x[:, t, :], x_d[0, t * P:(t + 1) * P, :]).then_inc(x_in[t], 16)
            for t in range(NT):
                sp.dma_start(pos_i[:, t:t + 1], pos_d[0, t * P:(t + 1) * P].rearrange("(p o) -> p o", o=1))\
                    .then_inc(pos_in, 16)

            def mixer_loads(layer):
                w = w_in_v[layer]
                base = MIX_BASE[layer]
                cols = {"q": (0, AW), "kv": (AW, QKV), "b": (QKV, QKV + CW), "c": (QKV + CW, QKV + 2 * CW),
                        "u": (QKV + 2 * CW, QKV + 3 * CW)}
                for name, _, buf, _ in MIX_UNITS:
                    if name in ("b", "out0", "out1"):
                        prev = {"b": "kv", "out0": "c", "out1": "u"}[name]
                        sp.wait_ge(lo_done, base + MIX_FIRST[prev])
                    elif layer == 1 and name in ("q", "c"):
                        h = DH - 2 if name == "q" else DH - 1
                        sp.wait_ge(lo_done, DENSE_BASE + gu_first(h) + 4)
                    if name.startswith("out"):
                        c = int(name[3])
                        for h in range(2):
                            sp.dma_start(unit[buf][:, 4 * h:4 * h + 4, :],
                                         w_out_v[layer, h, :, :, c * 512:(c + 1) * 512]).then_inc(unit_in[buf], 16)
                    else:
                        a, b = cols[name]
                        sp.dma_start(unit[buf][:, :, 0:b - a], w[:, :, a:b]).then_inc(unit_in[buf], 16)

            mixer_loads(0)
            base = MIX_BASE[0]
            blocks = (DH + 1) // 2

            def dense_down(j):
                if j < 2:
                    sp.wait_ge(mixlo_done, 8)
                else:
                    sp.wait_ge(lo_done, DENSE_BASE + d_first(2 * (j - 2) + 1, DH) + 2)
                n = min(4, 2 * (DH - 2 * j))
                sp.dma_start(raw_dv[:, j % 2, 0:n, :], dd_v[0, :, 4 * j:4 * j + n, :]).then_inc(down_in[j % 2], 16)

            for j in range(blocks):
                if j < 2:
                    sp.wait_ge(lo_done, base + [MIX_FIRST["out1"], MIX_PIECES][j])
                else:
                    sp.wait_ge(lo_done, DENSE_BASE + gu_first(2 * (j - 2) + 1) + 4)
                n = min(BLK, FD - j * BLK)
                for w, src in enumerate((dg_v, du_v)):
                    sp.dma_start(raw_gu[:, j % 2, w, :, 0:n], src[0, :, :, j * BLK:j * BLK + n])\
                        .then_inc(unit_in[2 * (j % 2) + w], 16)
                if j > 0:
                    dense_down(j - 1)
            dense_down(blocks - 1)
            mixer_loads(1)

            def expert_loads(first, e0, e1):
                for i, e in enumerate((e0, e1)):
                    for j in range(EB + 1):
                        s = (i * EB + j) % 2
                        here = first + i * E_PIECES
                        if j < EB:
                            h = 2 * j - 3
                            back = gu_first(h) + 4 if h >= 0 else gu_first(h + EH) + 4 - E_PIECES
                            sp.wait_ge(lo_done, here + back)
                            for w, src in enumerate((eg_v, eu_v)):
                                sp.dma_start(raw_gu[:, s, w, :, :], src[e, :, :, j * BLK:(j + 1) * BLK])\
                                    .then_inc(unit_in[2 * s + w], 16)
                        if j > 0:
                            h = 2 * (j - 1) - 3
                            back = d_first(h, EH) + 2 if h >= 0 else d_first(h + EH, EH) + 2 - E_PIECES
                            sp.wait_ge(lo_done, here + back)
                            sp.dma_start(raw_dv[:, 1 - s, :, :], ed_v[e, :, 4 * (j - 1):4 * j, :])\
                                .then_inc(down_in[1 - s], 16)

            sp.wait_ge(lo_done, MOE_BASE)
            sp.wait_ge(mixlo_done, 16)
            with sp.Fori(0, NE // 2) as pair:
                expert_loads(MOE_BASE + 2 * E_PIECES * pair, 2 * pair, 2 * pair + 1)

        @block.gpsimd
        def _(pool):
            n = 0

            def link(ins):
                nonlocal n
                n += 1
                ins.then_inc(pool_done, 1)

            link(nc.gpsimd.memset(ident[:, :], 0.0))
            pool.wait_ge(pool_done, n)
            nc.gpsimd.affine_select(out=ident[:, :], in_=ident[:, :], compare_op=ALU.not_equal, fill=1.0,
                                    base=0, pattern=[[-1, P]], channel_multiplier=1).then_inc(ident_done, 1)
            nc.gpsimd.dma_start(g_ffn[:, :, :], ffn_g.rearrange("l (p k) -> p l k", k=KT)).then_inc(consts_in, 16)
            nc.gpsimd.dma_start(g_att[:, :, :], att_g.rearrange("l (p k) -> p l k", k=4)).then_inc(consts_in, 16)
            nc.gpsimd.dma_start(g_conv[:, :, :], conv_g.rearrange("l (p k) -> p l k", k=CT)).then_inc(consts_in, 16)
            for layer in range(2):
                nc.gpsimd.dma_start(cw[:, layer], conv_w[layer].rearrange("w (p k) -> p w k", k=CT)).then_inc(consts_in, 16)
            nc.gpsimd.dma_start(sink_sb[:, :, :], sink.partition_broadcast(P)).then_inc(consts_in, 16)
            nc.gpsimd.dma_start(rout[:, :, :], router[0].rearrange("(p k) e -> p k e", k=KT)).then_inc(consts_in, 16)
            link(nc.gpsimd.memset(ones[:, :], 1.0))
            link(nc.gpsimd.memset(mask[:, :, :], 0.0))
            link(nc.gpsimd.memset(before[:, :], 1.0))
            link(nc.gpsimd.memset(eps[:, :], EPS))
            link(nc.gpsimd.memset(zeros[:, :].bitcast(F32), 0.0))
            nc.gpsimd.memset(gselT[:, :], 0.0).then_inc(gselT_out, 1)
            for e in range(NE):
                link(nc.gpsimd.memset(four_to[:, e:e + 1], float(4 ** e)))
            pool.wait_ge(pool_done, n)
            link(nc.gpsimd.affine_select(out=mask[:, 0, :], in_=mask[:, 0, :], compare_op=ALU.is_ge, fill=NEG,
                                         base=WINDOW, pattern=[[-1, SEQ]], channel_multiplier=1))
            link(nc.gpsimd.affine_select(out=mask[:, 1, :], in_=mask[:, 1, :], compare_op=ALU.is_ge, fill=NEG,
                                         base=WINDOW - P, pattern=[[1, SEQ]], channel_multiplier=-1))
            link(nc.gpsimd.affine_select(out=before[:, :], in_=before[:, :], compare_op=ALU.is_gt, fill=0.0,
                                         base=0, pattern=[[1, P]], channel_multiplier=-1))
            link(nc.gpsimd.iota(iota[:, :], [[1, SEQ]], base=0, channel_multiplier=0,
                                allow_small_or_imprecise_dtypes=True))
            assert n == POOL_STEPS
            nc.gpsimd.dma_start(gain_rows[:, :], ffn_g[1].partition_broadcast(P)).then_inc(gain_in, 16)
            pool.wait_ge(xg_done, 2)
            nc.gpsimd.dma_start(gain_rows[:, :], final_g.partition_broadcast(P)).then_inc(gain_in, 16)

        def wait_block_landed(eng, seen, B):
            for w in range(2):
                eng.wait_ge(unit_in[w], seen[w] + 16 + 16 * (B // 2))
                eng.wait_ge(unit_in[2 + w], seen[2 + w] + 16 * ((B + 1) // 2))

        @block.scalar
        def _(act):
            def copy(out, in_, **kw):
                return nc.scalar.activation(out, in_, ACT.Copy, **kw)

            def split_hi(n, src, ring, width=PW):
                if not isinstance(n, int) or n >= RING:
                    act.wait_ge(piece_used, n - RING + 1)
                out = hi[:, ring, 0:width]
                if len(src.shape) == 3:
                    out = out.rearrange("p (k c) -> p k c", k=src.shape[1])
                elif len(src.shape) == 4:
                    out = out.rearrange("p (k g c) -> p k g c", k=src.shape[1], g=src.shape[2])
                copy(out, src).then_inc(hi_done, 1)

            def mix_pieces(layer, a, b):
                for name, pieces, buf, _ in MIX_UNITS:
                    for q in range(pieces):
                        i = MIX_FIRST[name] + q
                        if a <= i < b:
                            if q == 0:
                                act.wait_ge(unit_in[buf], mix_landed[layer][name][1])
                            src = (unit[buf][:, 4 * q:4 * q + 4, 0:256] if name == "kv"
                                   else unit[buf][:, 2 * q:2 * q + 2, :])
                            n = MIX_BASE[layer] + i
                            split_hi(n, src, n % RING)

            def norm_stats(n, changed):
                halves = [(t, c) for c in range(2) for t in range(NT)] if n in (1, 3) else \
                    [(t, c) for t in range(NT) for c in range(2)]
                for i, (t, c) in enumerate(halves):
                    if n == 0:
                        act.wait_ge(x_in[t], 16)
                    else:
                        act.wait_ge(x_changed, changed - 3 + i)
                    half = slice(c * 512, (c + 1) * 512)
                    nc.scalar.activation(xn[:, t, half], x[:, t, half], ACT.Square,
                                         accum_out=ss_part[:, t, c:c + 1]).then_inc(sumsq_done, 1)
                act.wait_ge(ms_done, n + 1)
                nc.scalar.activation(std[:, :], ss[:, :], ACT.Sqrt).then_inc(std_done, 1)

            def norm_hi(n, gain, banks):
                if n == 1:
                    for w in range(2):
                        act.wait_ge(unit_in[w], dense_seen[w] + 16)
                    gu_pieces_hi(DENSE_BASE, DENSE_BASE, 0, 0, 0, 2)
                for b in range(4):
                    act.wait_ge(xT_done, 4 * n + b + 1)
                    for k in (2 * b, 2 * b + 1):
                        copy(act_hi[:, k, :], bank[banks[b]][:, (k % 2) * 256:(k % 2) * 256 + 256],
                             scale=gain[:, k:k + 1]).then_inc(xThi_done, 1)

            def exps(layer, t):
                act.wait_ge(masked_done, 2 * layer + t + 1)
                for h in range(NH):
                    nc.scalar.activation(prob[:, h * 256:(h + 1) * 256], prob[:, h * 256:(h + 1) * 256], ACT.Exp,
                                         bias=nmx[:, t, h:h + 1], accum_out=psums[:, t, h:h + 1]).then_inc(exp_done, 1)
                nc.scalar.activation(esink[:, t, :], sinkd[:, t, :], ACT.Exp).then_inc(exp_done, 1)

            def probT_copy(layer, t):
                act.wait_ge(probT_done, 2 * layer + t + 1)
                for b in range(2):
                    copy(probT[:, b * 512:(b + 1) * 512], bank[b][:, :]).then_inc(probT_out_a, 1)

            def mixer(layer):
                base = MIX_BASE[layer]
                pieces = lambda a, b: mix_pieces(layer, a, b)
                used = lambda i: act.wait_ge(piece_used, base + i + 1)
                if layer == 1:
                    pieces(0, 4)
                norm_stats(2 * layer, 8 * layer)
                if layer == 0:
                    act.wait_ge(gain0_in, 16)
                    pieces(0, 2)
                norm_hi(2 * layer, g_mix[:, layer, :], (0, 1, 2, 3))
                pieces(4 if layer else 2, 8)
                if layer == 0:
                    act.wait_ge(trig_arg, 1)
                    nc.scalar.activation(cs[:, :, :, :], turns[:, :, :, :], ACT.Sin).then_inc(trig_done, 1)
                pieces(8, 10)
                used(3)
                for t in range(NT):
                    copy(qkv[:, t, 0:AW].rearrange("p (c g d) -> p g c d", g=NKV, d=HD),
                         bank[4 + t][:, :].rearrange("p (g c d) -> p g c d", g=NKV, d=HD)).then_inc(qkv_out, 1)
                pieces(10, 12)
                used(5)
                for t in range(NT):
                    copy(qkv[:, t, AW:QKV], bank[6 + t][:, 0:256]).then_inc(qkv_out, 1)
                pieces(12, 14)
                used(9)
                for t in range(NT):
                    copy(z[:, t, :], bank[4 + t][:, :]).then_inc(c_out, 1)
                act.wait_ge(qkT_done, layer + 1)
                for b in range(2):
                    copy(qT[:, 2 * b:2 * b + 2, :], bank[b][:, :].rearrange("p (c n) -> p c n", c=2)).then_inc(qT_out, 1)
                pieces(14, 16)
                exps(layer, 0)
                pieces(16, 18)
                probT_copy(layer, 0)
                pieces(18, 22)
                exps(layer, 1)
                used(17)
                for t in range(NT):
                    copy(bb[:, t, :], bank[4 + t][:, :]).then_inc(b_out, 1)
                probT_copy(layer, 1)
                act.wait_ge(zT_done, layer + 1)
                for b in range(2):
                    copy(zT[:, 2 * b:2 * b + 2, 1:SEQ + 1],
                         bank[4 + b][:, :].rearrange("p (c n) -> p c n", c=2)).then_inc(zT_out, 1)
                pieces(22, 24)
                act.wait_ge(yc_done, layer + 1)
                nc.scalar.activation(sq, yc, ACT.Square).then_inc(sq_done, 1)
                for t in range(NT):
                    act.wait_ge(att_done, 2 * layer + t + 1)
                    nc.scalar.activation(prob[:, t * 512:(t + 1) * 512],
                                         att[:, t, :], ACT.Square,
                                         accum_out=ss_a[:, t:t + 1]).then_inc(attss_done, 1)
                act.wait_ge(attms_done, layer + 1)
                nc.scalar.activation(std_a[:, :], ss_a[:, :], ACT.Sqrt).then_inc(attstd_done, 1)
                if layer == 0:
                    act.wait_ge(consts_in, 16 * CONSTS)
                    act.wait_ge(pool_done, POOL_STEPS)
                act.wait_ge(cms_done, layer + 1)
                nc.scalar.activation(std_c, bank[2][:, 0:SEQ], ACT.Sqrt, bias=eps[:, 0:1],
                                     scale=1.0 / CW).then_inc(cstd_done, 1)
                act.wait_ge(attT_done, layer + 1)
                for k in range(4):
                    copy(act_hi[:, k, :], bank[k // 2][:, (k % 2) * 256:(k % 2) * 256 + 256],
                         scale=g_att[:, layer, k:k + 1]).then_inc(mixhi_done, 1)
                act.wait_ge(cn_done, layer + 1)
                for k in range(CT):
                    copy(act_hi[:, 4 + k, :], yc[:, k, :], scale=g_conv[:, layer, k:k + 1]).then_inc(mixhi_done, 1)
                pieces(24, 26)

            def gu_src(s, half, q):
                return raw_gu[:, s, :, 2 * q:2 * q + 2, half * HALF:(half + 1) * HALF].rearrange("p g k c -> p k g c")

            def down_piece_hi(first, ring, slot, half):
                for q in range(2):
                    split_hi(first + q, raw_dv[:, slot, 2 * half + q, :], (ring + q) % RING)

            def gu_pieces_hi(first, ring, slot, half, q0=0, q1=4):
                for q in range(q0, q1):
                    split_hi(first + q, gu_src(slot, half, q), (ring + q) % RING)

            def dense():
                b0 = DENSE_BASE

                def gu_landed(slot, count):
                    for w in range(2):
                        act.wait_ge(unit_in[2 * slot + w], dense_seen[2 * slot + w] + 16 * count)

                def silus(h, first, wait_free=True):
                    act.wait_ge(piece_used, first + 4)
                    if wait_free:
                        act.wait_ge(gated_done, h)
                    for t in range(NT):
                        ins = nc.scalar.activation(silu[:, t, :], bank[t][:, 0:HALF], ACT.Silu)
                    ins.then_inc(silu_done, 1)

                def turned(h):
                    act.wait_ge(gT_done, h + 1)
                    copy(at_hi[:, :], bank[2][:, :]).then_inc(atTh_done, 1)

                gu_pieces_hi(b0, b0, 0, 0, 2, 4)
                gu_pieces_hi(b0 + 4, b0 + 4, 0, 1, 0, 2)
                silus(0, b0, False)
                gu_pieces_hi(b0 + 4, b0 + 4, 0, 1, 2, 4)
                silus(1, b0 + 4)
                with act.Fori(0, 2) as i:
                    for j in (1, 2):
                        gu_landed(j % 2, i + 1 + j // 2)
                        for half in range(2):
                            h = 4 * i + 2 * j + half
                            first = act.snap(24 * i + (b0 + gu_first(2 * j + half)))
                            gu_pieces_hi(first, b0 + gu_first(2 * j + half), j % 2, half)
                            turned(h - 2)
                            if half == 0:
                                act.wait_ge(down_in[(j - 1) % 2], 16 * i + 16)
                            down_piece_hi(first + 4, b0 + gu_first(2 * j + half) + 4, (j - 1) % 2, half)
                            silus(h, first)
                h = DH - 1
                first = b0 + gu_first(h)
                gu_landed(1, 3)
                gu_pieces_hi(first, first, 1, 0)
                turned(h - 2)
                act.wait_ge(down_in[0], 48)
                down_piece_hi(first + 4, first + 4, 0, 0)
                silus(h, first)
                down_piece_hi(first + 6, first + 6, 0, 1)
                turned(h - 1)
                act.wait_ge(down_in[1], 48)
                down_piece_hi(first + 8, first + 8, 1, 0)
                turned(h)

            def experts(code):
                b0 = MOE_BASE

                def silu_of(half, n):
                    act.wait_ge(gated_done, n - 1)
                    nc.scalar.activation(silu[:, half, :], bank[half][:, 0:HALF], ACT.Silu).then_inc(silu_done, 1)

                def turned(half, n):
                    act.wait_ge(gT_done, n + 1)
                    copy(at_hi[:, half * 256:half * 256 + 256],
                         bank[2][:, half * 256:half * 256 + 256]).then_inc(atTh_done, 1)

                def down_landed(B):
                    act.wait_ge(down_in[0], DOWN0 + 16 + 16 * (B // 2))
                    act.wait_ge(down_in[1], DOWN0 + 16 * ((B + 1) // 2))

                def gather_hi(p):
                    act.wait_ge(gathered, p + 1)
                    for b in range(2):
                        copy(act_hi[:, 4 * b:4 * b + 4, 0:P],
                             bank[5 + b][:, :].rearrange("p (k n) -> p k n", k=4)).then_inc(xehi_done, 1)

                def rows_out(p):
                    act.wait_ge(scattered, 4 * p + 1)
                    act.wait_ge(piece_used, b0 + E_PIECES * p)
                    copy(y[:, 0:512], bank[3][:, :]).then_inc(y_act, 1)

                def one_tile(p, first, n0, B0, s0):
                    wait_block_landed(act, moe_seen, B0)
                    gu_pieces_hi(first, b0, s0, 0)
                    rows_out(p)
                    gu_pieces_hi(first + 4, b0 + 4, s0, 1)
                    act.wait_ge(piece_used, first + 4)
                    silu_of(0, n0)
                    with act.Fori(1, EB) as j:
                        f = act.snap(first + 12 * j - 4)
                        n = act.snap(n0 + 2 * j)
                        B = act.snap(B0 + j)
                        s = act.snap(B % 2)
                        wait_block_landed(act, moe_seen, B)
                        gu_pieces_hi(f, b0 + 8, s, 0)
                        turned(0, n - 2)
                        silu_of(1, n - 1)
                        down_landed(B - 1)
                        down_piece_hi(f + 4, b0 + 12, 1 - s, 0)
                        gu_pieces_hi(f + 6, b0 + 14, s, 1)
                        turned(1, n - 1)
                        silu_of(0, n)
                        down_piece_hi(f + 10, b0 + 18, 1 - s, 1)
                    f = act.snap(first + d_first(EH - 2, EH))
                    n = act.snap(n0 + EH)
                    turned(0, n - 2)
                    silu_of(1, n - 1)
                    down_landed(B0 + EB - 1)
                    down_piece_hi(f, b0 + 8, s0, 0)
                    gather_hi(p + 1)
                    act.wait_ge(gselT_done, p + 1)
                    copy(gselT[:, :], bank[7][:, 0:SEQ]).then_inc(gselT_out, 1)
                    turned(1, n - 1)
                    down_piece_hi(f + 2, b0 + 10, s0, 1)

                def two_tiles(p, first, n0, B0, s0, u):
                    def silus(n, used_to):
                        act.wait_ge(piece_used, used_to)
                        act.wait_ge(gated_done, n)
                        for t in range(NT):
                            ins = nc.scalar.activation(silu[:, t, :], bank[t][:, 0:HALF], ACT.Silu)
                        ins.then_inc(silu_done, 1)

                    def turned_both(n):
                        act.wait_ge(gT_done, n + 1)
                        copy(at_hi[:, :], bank[2][:, :]).then_inc(atTh_done, 1)

                    wait_block_landed(act, moe_seen, B0)
                    rows_out(p)
                    gu_pieces_hi(first, b0, s0, 0, 0, 2)
                    act.wait_ge(gathered2, u + 1)
                    for b in range(2):
                        copy(act_hi[:, 4 * b:4 * b + 4, P:SEQ],
                             bank[5 + b][:, :].rearrange("p (k n) -> p k n", k=4)).then_inc(xehi2_done, 1)
                    gu_pieces_hi(first, b0, s0, 0, 2, 4)
                    gu_pieces_hi(first + 4, b0 + 4, s0, 1, 0, 2)
                    silus(n0, first + 4)
                    gu_pieces_hi(first + 4, b0 + 4, s0, 1, 2, 4)
                    silus(n0 + 1, first + 8)
                    with act.Fori(1, EB) as j:
                        f = act.snap(first + 12 * j - 4)
                        n = act.snap(n0 + 2 * j)
                        B = act.snap(B0 + j)
                        s = act.snap(B % 2)
                        for half in range(2):
                            if half == 0:
                                wait_block_landed(act, moe_seen, B)
                            gu_pieces_hi(f + 6 * half, b0 + 8 + 6 * half, s, half)
                            turned_both(n + half - 2)
                            if half == 0:
                                down_landed(B - 1)
                            down_piece_hi(f + 6 * half + 4, b0 + 12 + 6 * half, 1 - s, half)
                            silus(n + half, f + 6 * half + 4)
                    f = act.snap(first + d_first(EH - 2, EH))
                    n = act.snap(n0 + EH)
                    down_landed(B0 + EB - 1)
                    down_piece_hi(f, b0 + 8, s0, 0)
                    turned_both(n - 2)
                    down_piece_hi(f + 2, b0 + 10, s0, 1)
                    turned_both(n - 1)
                    act.wait_ge(gselT2_done, u + 1)
                    copy(gselT[:, :], bank[7][:, 0:SEQ]).then_inc(gselT2_out, 1)
                    act.wait_ge(piece_used, first + E_PIECES)
                    copy(y[:, 0:512], bank[5][:, :]).then_inc(y2_act, 1)
                    gather_hi(p + 1)
                    act.wait_ge(gselT_done, p + 1)
                    copy(gselT[:, :], bank[7][:, 0:SEQ]).then_inc(gselT_out, 1)

                gather_hi(0)
                with act.Fori(0, NE) as p:
                    first = act.snap(b0 + E_PIECES * p)
                    n0 = act.snap(DH + EH * p)
                    B0 = act.snap(EB * p)
                    s0 = act.snap(p % 2)
                    v = act.snap((code >> (2 * p)) & 3, min_val=0, max_val=3)
                    with act.If(v > 0):
                        two_tiles(p, first, n0, B0, s0, act.snap((v + 3) & 3, min_val=0, max_val=3))
                    with act.Else():
                        one_tile(p, first, n0, B0, s0)
                rows_out(NE)

            nc.scalar.dma_start(g_mix[:, :, :], mix_g.rearrange("l (p k) -> p l k", k=KT)).then_inc(gain0_in, 16)
            mixer(0)
            norm_stats(1, 4)
            norm_hi(1, g_ffn[:, 0, :], (3, 4, 5, 6))
            dense()
            mixer(1)
            norm_stats(3, 12)
            copy(rout_hl[:, :, 0:NE], rout[:, :, :]).then_inc(routhi_done, 1)
            norm_hi(3, g_ffn[:, 1, :], (3, 4, 5, 6))
            act.wait_ge(gdiff_done, 1)
            nc.scalar.activation(gexp[:, :], gdiff[:, :], ACT.Exp).then_inc(gexp_done, 1)
            act.wait_ge(plan_done, 1)
            experts(act.value_load(plan[0:1, 0:1], min_val=0, max_val=65535))
            nc.scalar.activation(table_warm[:, :], eps[:, :], ACT.Sqrt)
            for t in range(NT):
                act.wait_ge(x_changed, 12 + 4 * NE + 2 * (t + 1))
                nc.scalar.activation(xn[:, t, :], x[:, t, :], ACT.Square,
                                     accum_out=ss[:, t:t + 1]).then_inc(sumsq_done, 1)
                act.wait_ge(ms_done, 5 + t)
                nc.scalar.activation(std[:, t:t + 1], ss[:, t:t + 1], ACT.Sqrt).then_inc(std_done, 1)
            for t in range(NT):
                act.wait_ge(final_done, t + 1)
                nc.scalar.dma_start(out_d[0, t * P:(t + 1) * P, :], xn[:, t, :]).then_inc(stored, 16)
            act.wait_ge(stored, 32)

        @block.vector
        def _(dve):
            steps = [0]

            def link(ins):
                steps[0] += 1
                ins.then_inc(dve_step, 1)
                dve.wait_ge(dve_step, steps[0])

            v = nc.vector

            def split_lo(n, src, ring, width=PW):
                dve.wait_ge(hi_done, n + 1)
                out, h = lo[:, ring, 0:width], hi[:, ring, 0:width]
                if len(src.shape) == 3:
                    out, h = (a.rearrange("p (k c) -> p k c", k=src.shape[1]) for a in (out, h))
                elif len(src.shape) == 4:
                    out, h = (a.rearrange("p (k g c) -> p k g c", k=src.shape[1], g=src.shape[2]) for a in (out, h))
                v.tensor_tensor(out, src, h, ALU.subtract).then_inc(lo_done, 1)

            def mix_pieces(layer, a, b):
                for name, pieces, buf, _ in MIX_UNITS:
                    for q in range(pieces):
                        i = MIX_FIRST[name] + q
                        if a <= i < b:
                            src = (unit[buf][:, 4 * q:4 * q + 4, 0:256] if name == "kv"
                                   else unit[buf][:, 2 * q:2 * q + 2, :])
                            n = MIX_BASE[layer] + i
                            split_lo(n, src, n % RING)

            def norm_scale(n):
                dve.wait_ge(sumsq_done, 4 * (n + 1))
                link(v.tensor_tensor(ss[:, :], ss_part[:, :, 0], ss_part[:, :, 1], ALU.add))
                v.tensor_scalar(ss[:, :], ss[:, :], 1.0 / D, EPS, ALU.mult, ALU.add).then_inc(ms_done, 1)
                dve.wait_ge(std_done, n + 1)
                link(v.reciprocal(rstd[:, :], std[:, :]))
                for t in range(NT):
                    v.tensor_scalar(xn[:, t, :], x[:, t, :], rstd[:, t:t + 1], None, ALU.mult).then_inc(xn_done, 1)

            def norm_lo(n, gain, banks):
                if n == 1:
                    gu_pieces_lo(DENSE_BASE, DENSE_BASE, 0, 0, 0, 2)
                for k in range(KT):
                    dve.wait_ge(xThi_done, KT * n + 2 * (k // 2) + 2)
                    v.scalar_tensor_tensor(out=act_lo[:, k, :], in0=bank[banks[k // 2]][:, (k % 2) * 256:(k % 2) * 256 + 256],
                                           scalar=gain[:, k:k + 1], in1=act_hi[:, k, :],
                                           op0=ALU.mult, op1=ALU.subtract).then_inc(xTlo_done, 1)

            def rope_angles():
                freq = np.float32(THETA) ** (-np.arange(0, ROT, 2, dtype=np.float32) / np.float32(ROT))
                for j in range(HR):
                    ins = v.memset(inv_freq[:, j:j + 1], float(freq[j]))
                link(ins)
                dve.wait_ge(pos_in, 16 * NT)
                link(v.tensor_copy(pos_f[:, :], pos_i[:, :]))
                shape = [P, NT, HR]
                link(v.tensor_tensor(ang[:, :, :], pos_f[:, :].unsqueeze(2).to_broadcast(shape),
                                     inv_freq[:, :].unsqueeze(1).to_broadcast(shape), ALU.mult))
                big = 1.5 * 2.0 ** 23
                two_pi = 2 * np.pi
                c1 = 6.28125
                c2 = float(np.floor((two_pi - c1) * 2 ** 16) / 2 ** 16)
                c3 = two_pi - c1 - c2
                for f, quarter in ((0, 0.25), (1, 0.0)):
                    w = turns[:, f]
                    link(v.tensor_scalar(w, ang[:, :, :], 1.0 / two_pi, quarter, ALU.mult, ALU.add))
                    link(v.tensor_scalar(w, w, big, None, ALU.add))
                    link(v.tensor_scalar(w, w, big, None, ALU.subtract))
                    r = cs[:, f]
                    link(v.scalar_tensor_tensor(out=r, in0=w, scalar=-c1, in1=ang[:, :, :], op0=ALU.mult, op1=ALU.add))
                    link(v.scalar_tensor_tensor(out=r, in0=w, scalar=-c2, in1=r, op0=ALU.mult, op1=ALU.add))
                    link(v.scalar_tensor_tensor(out=r, in0=w, scalar=-c3, in1=r, op0=ALU.mult, op1=ALU.add))
                    if f == 0:
                        link(v.tensor_scalar(r, r, float(np.pi / 2), None, ALU.add))
                    ins = v.tensor_scalar(w, r, 3.1415925, -3.1415925, ALU.min, ALU.max)
                ins.then_inc(trig_arg, 1)

            def rope(layer):
                dve.wait_ge(qkv_out, 4 * (layer + 1))
                if layer == 0:
                    dve.wait_ge(consts_in, 16 * CONSTS)
                    dve.wait_ge(pool_done, POOL_STEPS)
                    dve.wait_ge(trig_done, 1)
                heads = qkv[:, :, 0:AW + KVW].rearrange("p t (h d) -> p t h d", d=HD)
                x1, x2 = heads[:, :, :, 0:HR], heads[:, :, :, HR:ROT]
                shape = [P, NT, NH + NKV, HR]
                for t in range(NT):
                    cos = cs[:, 0, t].unsqueeze(1).to_broadcast([P, NH + NKV, HR])
                    sin = cs[:, 1, t].unsqueeze(1).to_broadcast([P, NH + NKV, HR])
                    for f, (a, b) in enumerate(((x1, cos), (x2, sin), (x2, cos), (x1, sin))):
                        ins = v.tensor_tensor(rope_t[:, f, t], a[:, t], b, ALU.mult)
                link(ins)
                v.tensor_tensor(x1, rope_t[:, 0], rope_t[:, 1], ALU.subtract)
                v.tensor_tensor(x2, rope_t[:, 2], rope_t[:, 3], ALU.add).then_inc(rope_done, 1)

            def masked_scores(layer, t):
                i = 2 * layer + t
                for b in range(4):
                    dve.wait_ge(scores_done, 4 * i + b + 1)
                    two_heads = prob[:, b * 512:(b + 1) * 512].rearrange("p (h n) -> p h n", h=2)
                    link(v.scalar_tensor_tensor(
                        out=two_heads, in0=bank[b][:, :].rearrange("p (h n) -> p h n", h=2), scalar=HD ** -0.5,
                        in1=mask[:, t, :].unsqueeze(1).to_broadcast([P, 2, SEQ]), op0=ALU.mult, op1=ALU.add))
                    ins = v.tensor_reduce(mx[:, 2 * b:2 * b + 2], two_heads, AX, ALU.max)
                link(ins)
                link(v.tensor_tensor(mx[:, :], mx[:, :], sink_sb[:, layer, :], ALU.max))
                v.tensor_scalar(nmx[:, t, :], mx[:, :], -1.0, None, ALU.mult)
                v.tensor_tensor(sinkd[:, t, :], sink_sb[:, layer, :], mx[:, :], ALU.subtract).then_inc(masked_done, 1)

            def denominators(layer, t):
                dve.wait_ge(exp_done, (NH + 1) * (2 * layer + t + 1))
                link(v.tensor_tensor(den[:, t, :], psums[:, t, :], esink[:, t, :], ALU.add))
                v.reciprocal(rden[:, t, :], den[:, t, :]).then_inc(rden_done, 1)

            def probT_copy(layer, t):
                dve.wait_ge(probT_done, 2 * layer + t + 1)
                for b in range(2, 4):
                    v.tensor_copy(probT[:, b * 512:(b + 1) * 512], bank[b][:, :]).then_inc(probT_out_v, 1)

            def attended(layer, t):
                dve.wait_ge(av_done, 2 * layer + t + 1)
                dve.wait_ge(rden_done, 2 * layer + t + 1)
                v.tensor_tensor(att[:, t, :].rearrange("p (h d) -> p h d", h=NH),
                                bank[6 + t][:, :].rearrange("p (h d) -> p h d", h=NH),
                                rden[:, t, :].unsqueeze(2).to_broadcast([P, NH, HD]), ALU.mult).then_inc(att_done, 1)

            def mixer(layer):
                base = MIX_BASE[layer]
                pieces = lambda a, b: mix_pieces(layer, a, b)
                if layer == 0:
                    dve.wait_ge(gain0_in, 16)
                else:
                    dve.wait_ge(lo_done, MIX_BASE[1])
                norm_scale(2 * layer)
                if layer == 0:
                    pieces(0, 2)
                norm_lo(2 * layer, g_mix[:, layer, :], (0, 1, 2, 3))
                v.memset(zT[:, :, 0:1], 0.0)
                link(v.memset(zT[:, :, SEQ + 1:SEQ + 2], 0.0))
                pieces(4 if layer else 2, 8)
                if layer == 0:
                    rope_angles()
                pieces(8, 12)
                rope(layer)
                pieces(12, 14)
                dve.wait_ge(qkT_done, layer + 1)
                v.tensor_copy(kT, bank[2][:, 0:SEQ]).then_inc(kT_out, 1)
                pieces(14, 16)
                masked_scores(layer, 0)
                pieces(16, 18)
                dve.wait_ge(c_out, 2 * (layer + 1))
                dve.wait_ge(piece_used, base + MIX_FIRST["b"])
                for t in range(NT):
                    v.tensor_tensor(z[:, t, :], z[:, t, :], bank[6 + t][:, :], ALU.mult).then_inc(z_done, 1)
                denominators(layer, 0)
                probT_copy(layer, 0)
                pieces(18, 22)
                masked_scores(layer, 1)
                attended(layer, 0)
                probT_copy(layer, 1)
                denominators(layer, 1)
                dve.wait_ge(zT_out, 2 * (layer + 1))
                for k in range(CT):
                    ins = v.tensor_scalar(yc[:, k, :], zT[:, k, 0:SEQ], cw[:, layer, 0, k:k + 1], None, ALU.mult)
                link(ins)
                for w in (1, 2):
                    for k in range(CT):
                        ins = v.scalar_tensor_tensor(out=yc[:, k, :], in0=zT[:, k, w:w + SEQ],
                                                     scalar=cw[:, layer, w, k:k + 1], in1=yc[:, k, :],
                                                     op0=ALU.mult, op1=ALU.add)
                    link(ins)
                dve.wait_ge(bT_done, layer + 1)
                for b in range(2):
                    c = slice(2 * b, 2 * b + 2)
                    ins = v.tensor_tensor(yc[:, c, :], yc[:, c, :], bank[4 + b][:, :].rearrange("p (c n) -> p c n", c=2),
                                          ALU.mult)
                ins.then_inc(yc_done, 1)
                attended(layer, 1)
                dve.wait_ge(attss_done, 2 * (layer + 1))
                v.tensor_scalar(ss_a[:, :], ss_a[:, :], 1.0 / AW, EPS, ALU.mult, ALU.add).then_inc(attms_done, 1)
                pieces(22, 24)
                dve.wait_ge(attstd_done, layer + 1)
                link(v.reciprocal(rstd_a[:, :], std_a[:, :]))
                for t in range(NT):
                    ins = v.tensor_scalar(att[:, t, :], att[:, t, :], rstd_a[:, t:t + 1], None, ALU.mult)
                ins.then_inc(attn_done, 1)
                dve.wait_ge(cstd_done, layer + 1)
                link(v.reciprocal(rstd_c, std_c))
                v.tensor_tensor(yc, yc, rstd_c.unsqueeze(1).to_broadcast([P, CT, SEQ]), ALU.mult).then_inc(cn_done, 1)
                for k in range(KT):
                    dve.wait_ge(mixhi_done, 8 * layer + (k + 1 if k >= 4 else k // 2 * 2 + 2))
                    if k >= 4:
                        src, g = yc[:, k - 4, :], g_conv[:, layer, k - 4:k - 3]
                    else:
                        src, g = bank[k // 2][:, (k % 2) * 256:(k % 2) * 256 + 256], g_att[:, layer, k:k + 1]
                    v.scalar_tensor_tensor(out=act_lo[:, k, :], in0=src, scalar=g, in1=act_hi[:, k, :],
                                           op0=ALU.mult, op1=ALU.subtract).then_inc(mixlo_done, 1)
                pieces(24, 26)
                for c, name in enumerate(("out0", "out1")):
                    dve.wait_ge(piece_used, base + MIX_FIRST[name] + 4)
                    for t in range(NT):
                        xs = x[:, t, c * 512:(c + 1) * 512]
                        v.tensor_tensor(xs, xs, bank[4 + 2 * c + t][:, :], ALU.add).then_inc(x_changed, 1)

            def gu_src(s, half, q):
                return raw_gu[:, s, :, 2 * q:2 * q + 2, half * HALF:(half + 1) * HALF].rearrange("p g k c -> p k g c")

            def gu_pieces_lo(first, ring, slot, half, q0=0, q1=4):
                for q in range(q0, q1):
                    split_lo(first + q, gu_src(slot, half, q), (ring + q) % RING)

            def down_pieces_lo(first, ring, slot, half):
                for q in range(2):
                    split_lo(first + q, raw_dv[:, slot, 2 * half + q, :], (ring + q) % RING)

            def dense():
                b0 = DENSE_BASE

                def gate(h, half, wait_free=True):
                    dve.wait_ge(silu_done, h + 1)
                    for t in range(NT):
                        ins = v.tensor_tensor(gated[:, 2 * half + t, :], silu[:, t, :], bank[t][:, HALF:BLK], ALU.mult)
                    ins.then_inc(gated_done, 1)

                def turned(h):
                    dve.wait_ge(atTh_done, h + 1)
                    v.tensor_tensor(at_lo[:, :], bank[2][:, :], at_hi[:, :], ALU.subtract).then_inc(atTl_done, 1)

                gu_pieces_lo(b0, b0, 0, 0, 2, 4)
                gu_pieces_lo(b0 + 4, b0 + 4, 0, 1, 0, 2)
                gate(0, 0)
                gu_pieces_lo(b0 + 4, b0 + 4, 0, 1, 2, 4)
                gate(1, 1)
                with dve.Fori(0, 2) as i:
                    for j in (1, 2):
                        for half in range(2):
                            h = 4 * i + 2 * j + half
                            ring = b0 + gu_first(2 * j + half)
                            first = dve.snap(24 * i + ring)
                            gu_pieces_lo(first, ring, j % 2, half)
                            turned(h - 2)
                            down_pieces_lo(first + 4, ring + 4, (j - 1) % 2, half)
                            gate(h, half)
                h = DH - 1
                first = b0 + gu_first(h)
                gu_pieces_lo(first, first, 1, 0)
                turned(h - 2)
                down_pieces_lo(first + 4, first + 4, 0, 0)
                gate(h, 0)
                down_pieces_lo(first + 6, first + 6, 0, 1)
                turned(h - 1)
                down_pieces_lo(first + 8, first + 8, 1, 0)
                turned(h)
                mix_pieces(1, 0, 4)
                dve.wait_ge(piece_used, b0 + D_PIECES)
                for t in range(NT):
                    for c in range(2):
                        xs = x[:, t, c * 512:(c + 1) * 512]
                        v.tensor_tensor(xs, xs, bank[3 + 2 * t + c][:, :], ALU.add).then_inc(x_changed, 1)

            def route():
                dve.wait_ge(routhi_done, 1)
                v.tensor_tensor(rout_hl[:, :, NE:2 * NE], rout[:, :, :], rout_hl[:, :, 0:NE], ALU.subtract).then_inc(routlo_done, 1)
                norm_lo(3, g_ffn[:, 1, :], (3, 4, 5, 6))
                dve.wait_ge(gain_in, 16)
                v.tensor_tensor(xn[:, 0, :], xn[:, 0, :], gain_rows[:, :], ALU.mult).then_inc(xg_done, 1)
                dve.wait_ge(logT_done, 1)
                v.tensor_copy(logT, bank[2][0:2 * NE, 0:SEQ]).then_inc(logT_out, 1)
                v.tensor_tensor(xn[:, 1, :], xn[:, 1, :], gain_rows[:, :], ALU.mult).then_inc(xg_done, 1)
                dve.wait_ge(logits_done, 1)
                link(v.tensor_copy(gsum[:, :, :, :].rearrange("p h t e -> p t h e"),
                                   bank[7][:, 0:NT * 2 * NE].rearrange("p (t h e) -> p t h e", t=NT, h=2)))
                link(v.tensor_tensor(logit[:, :, :], gsum[:, 0], gsum[:, 1], ALU.add))
                for t in range(NT):
                    ins = v.max(top[:, t, :], logit[:, t, :])
                link(ins)
                v.tensor_tensor(gdiff[:, :], top[:, :, 1], top[:, :, 0], ALU.subtract).then_inc(gdiff_done, 1)
                for t in range(NT):
                    ins = v.max_index(topi[:, t, :], top[:, t, :], logit[:, t, :])
                link(ins)
                link(v.tensor_copy(topf[:, :, :], topi[:, :, 0:2]))
                for c in range(2):
                    for t in range(NT):
                        ins = v.tensor_scalar(oneh[:, c, t, :], iota[:, 0:NE], topf[:, t, c:c + 1], None, ALU.is_equal)
                link(ins)
                v.tensor_tensor(chosen[:, :, :], oneh[:, 0], oneh[:, 1], ALU.add).then_inc(chosen_done, 1)
                dve.wait_ge(gexp_done, 1)
                link(v.tensor_scalar(gden[:, :], gexp[:, :], 1.0, None, ALU.add))
                link(v.reciprocal(gates[:, :, 0], gden[:, :]))
                link(v.tensor_tensor(gates[:, :, 1], gates[:, :, 0], gexp[:, :], ALU.mult))
                for c in range(2):
                    for t in range(NT):
                        ins = v.tensor_scalar(gsum[:, c, t, :], oneh[:, c, t, :], gates[:, t, c:c + 1], None, ALU.mult)
                link(ins)
                by_expert = slot_of[:, 0:NE, :].rearrange("p e t -> p t e")
                gate_by_expert = gate_of[:, 0:NE, :].rearrange("p e t -> p t e")
                v.memset(slot_of[:, NE:NCOL, :], -1.0)
                v.memset(gate_of[:, NE:NCOL, :], 0.0)
                v.tensor_tensor(gate_by_expert, gsum[:, 0], gsum[:, 1], ALU.add)
                dve.wait_ge(rank_done, 1)
                ranks = bank[7][:, 0:NT * NE].rearrange("p (t e) -> p t e", t=NT)
                link(v.scalar_tensor_tensor(out=rank1[:, :, :], in0=ranks, scalar=1.0, in1=chosen[:, :, :],
                                            op0=ALU.add, op1=ALU.mult))
                link(v.tensor_scalar(by_expert, rank1[:, :, :], 1.0, None, ALU.subtract))
                counts = bank[7][:, NT * NE:NT * NE + NE]
                link(v.tensor_scalar(over[:, 0, :], counts, float(P) + 0.5, None, ALU.is_ge))
                src = 0
                for i, shift in enumerate((1, 2, 4)):
                    v.tensor_copy(over[:, i + 1, 0:shift], over[:, src, 0:shift])
                    link(v.tensor_tensor(over[:, i + 1, shift:NE], over[:, src, shift:NE],
                                         over[:, src, 0:NE - shift], ALU.add))
                    src = i + 1
                link(v.tensor_tensor(two[:, :], over[:, 0, :], over[:, 3, :], ALU.mult))
                link(v.tensor_tensor(two[:, :], two[:, :], four_to[:, :], ALU.mult))
                link(v.tensor_reduce(plan_f[:, :], two[:, :], AX, ALU.add))
                v.tensor_copy(plan[:, :], plan_f[:, :]).then_inc(plan_done, 1)

            def build_sel(p, tile=0, done=sel_done):
                for t in range(NT):
                    ins = v.tensor_scalar(sel[:, t, :], iota[:, tile * P:(tile + 1) * P], slot_of[:, p, t:t + 1],
                                          None, ALU.is_equal)
                ins.then_inc(done, 1)

            def build_gsel(p, out=gsel, tile=0, done=gsel_done):
                for t in range(NT):
                    ins = v.tensor_scalar(out[:, t, :], iota[:, tile * P:(tile + 1) * P], slot_of[:, p, t:t + 1],
                                          gate_of[:, p, t:t + 1], ALU.is_equal, ALU.mult)
                ins.then_inc(done, 1)

            def experts():
                b0 = MOE_BASE

                def gate(half, n):
                    dve.wait_ge(silu_done, n + 1)
                    v.tensor_tensor(gated[:, half, :], silu[:, half, :], bank[half][:, HALF:BLK], ALU.mult)\
                        .then_inc(gated_done, 1)

                def turned(half, n):
                    dve.wait_ge(atTh_done, n + 1)
                    c = slice(half * 256, half * 256 + 256)
                    v.tensor_tensor(at_lo[:, c], bank[2][:, c], at_hi[:, c], ALU.subtract).then_inc(atTl_done, 1)

                def gather_lo(p):
                    for b in range(2):
                        dve.wait_ge(xehi_done, 2 * p + b + 1)
                        v.tensor_tensor(act_lo[:, 4 * b:4 * b + 4, 0:P],
                                        bank[5 + b][:, :].rearrange("p (k n) -> p k n", k=4),
                                        act_hi[:, 4 * b:4 * b + 4, 0:P], ALU.subtract).then_inc(xelo_done, 1)

                def rows_out(p):
                    dve.wait_ge(scattered, 4 * p + 1)
                    dve.wait_ge(piece_used, b0 + E_PIECES * p)
                    v.tensor_copy(y[:, 512:D], bank[4][:, :]).then_inc(y_dve, 1)

                def add_rows(p, r0=0, r1=4):
                    if r0 == 0:
                        dve.wait_ge(x_changed, 12 + 4 * p)
                    for r in range(r0, r1):
                        t, c, b = r // 2, r % 2, (5, 6, 7, 5)[r]
                        dve.wait_ge(scattered, 4 * p + r + 2)
                        xs = x[:, t, c * 512:(c + 1) * 512]
                        v.tensor_tensor(xs, xs, bank[b][:, :], ALU.add).then_inc(x_changed, 1)

                build_sel(0)
                build_gsel(0)

                def one_tile(p, first, n0, s0):
                    gu_pieces_lo(first, b0, s0, 0)
                    rows_out(p)
                    for q in range(4):
                        split_lo(first + 4 + q, gu_src(s0, 1, q), (b0 + 4 + q) % RING)
                        if q == 1:
                            add_rows(p, 0, 1)
                    add_rows(p, 1, 4)
                    gate(0, n0)
                    dve.wait_ge(gathered, p + 1)
                    build_sel(p + 1)
                    with dve.Fori(1, EB) as j:
                        f = dve.snap(first + 12 * j - 4)
                        n = dve.snap(n0 + 2 * j)
                        s = dve.snap((p + j) % 2)
                        s1 = dve.snap((p + j + 1) % 2)
                        gu_pieces_lo(f, b0 + 8, s, 0)
                        turned(0, n - 2)
                        gate(1, n - 1)
                        down_pieces_lo(f + 4, b0 + 12, s1, 0)
                        gu_pieces_lo(f + 6, b0 + 14, s, 1)
                        turned(1, n - 1)
                        gate(0, n)
                        down_pieces_lo(f + 10, b0 + 18, s1, 1)
                    f = dve.snap(first + d_first(EH - 2, EH))
                    n = dve.snap(n0 + EH)
                    turned(0, n - 2)
                    gate(1, n - 1)
                    down_pieces_lo(f, b0 + 8, s0, 0)
                    gather_lo(p + 1)
                    turned(1, n - 1)
                    down_pieces_lo(f + 2, b0 + 10, s0, 1)
                    dve.wait_ge(gselT_done, p + 1)
                    build_gsel(p + 1)

                def two_tiles(p, first, n0, s0, u):
                    def gate_both(n, half):
                        dve.wait_ge(silu_done, n + 1)
                        for t in range(NT):
                            ins = vec.tensor_tensor(gated[:, 2 * half + t, :], silu[:, t, :], bank[t][:, HALF:BLK],
                                                    ALU.mult)
                        ins.then_inc(gated_done, 1)

                    def turned_both(n):
                        dve.wait_ge(atTh_done, n + 1)
                        vec.tensor_tensor(at_lo[:, :], bank[2][:, :], at_hi[:, :], ALU.subtract).then_inc(atTl_done, 1)

                    dve.wait_ge(gathered, p + 1)
                    build_sel(p, 1, sel2_done)
                    build_gsel(p, gsel2, 1, gsel2_done)
                    rows_out(p)
                    gu_pieces_lo(first, b0, s0, 0, 0, 2)
                    for b in range(2):
                        dve.wait_ge(xehi2_done, 2 * u + b + 1)
                        vec.tensor_tensor(act_lo[:, 4 * b:4 * b + 4, P:SEQ],
                                          bank[5 + b][:, :].rearrange("p (k n) -> p k n", k=4),
                                          act_hi[:, 4 * b:4 * b + 4, P:SEQ], ALU.subtract).then_inc(xelo2_done, 1)
                    gu_pieces_lo(first, b0, s0, 0, 2, 4)
                    gu_pieces_lo(first + 4, b0 + 4, s0, 1, 0, 2)
                    gate_both(n0, 0)
                    add_rows(p, 0, 1)
                    gu_pieces_lo(first + 4, b0 + 4, s0, 1, 2, 4)
                    add_rows(p, 1, 4)
                    build_sel(p + 1)
                    gate_both(n0 + 1, 1)
                    with dve.Fori(1, EB) as j:
                        f = dve.snap(first + 12 * j - 4)
                        n = dve.snap(n0 + 2 * j)
                        s = dve.snap((p + j) % 2)
                        s1 = dve.snap((p + j + 1) % 2)
                        for half in range(2):
                            gu_pieces_lo(f + 6 * half, b0 + 8 + 6 * half, s, half)
                            turned_both(n + half - 2)
                            down_pieces_lo(f + 6 * half + 4, b0 + 12 + 6 * half, s1, half)
                            gate_both(n + half, half)
                    f = dve.snap(first + d_first(EH - 2, EH))
                    n = dve.snap(n0 + EH)
                    down_pieces_lo(f, b0 + 8, s0, 0)
                    turned_both(n - 2)
                    down_pieces_lo(f + 2, b0 + 10, s0, 1)
                    turned_both(n - 1)
                    dve.wait_ge(piece_used, first + E_PIECES)
                    vec.tensor_copy(y[:, 512:D], bank[6][:, :]).then_inc(y2_dve, 1)
                    for r, b in enumerate((0, 1, 2, 7)):
                        t, c = r // 2, r % 2
                        dve.wait_ge(scattered2, 4 * u + r + 1)
                        xs = x[:, t, c * 512:(c + 1) * 512]
                        vec.tensor_tensor(xs, xs, bank[b][:, :], ALU.add).then_inc(x_changed2, 1)
                    gather_lo(p + 1)
                    dve.wait_ge(gselT_done, p + 1)
                    build_gsel(p + 1)

                vec = nc.vector
                dve.wait_ge(plan_done, 1)
                code = dve.value_load(plan[0:1, 0:1], min_val=0, max_val=65535)
                gather_lo(0)
                with dve.Fori(0, NE) as p:
                    first = dve.snap(b0 + E_PIECES * p)
                    n0 = dve.snap(DH + EH * p)
                    s0 = dve.snap(p % 2)
                    number = dve.snap((code >> (2 * p)) & 3, min_val=0, max_val=3)
                    with dve.If(number > 0):
                        two_tiles(p, first, n0, s0, dve.snap((number + 3) & 3, min_val=0, max_val=3))
                    with dve.Else():
                        one_tile(p, first, n0, s0)
                rows_out(NE)
                add_rows(NE)

            mixer(0)
            norm_scale(1)
            norm_lo(1, g_ffn[:, 0, :], (3, 4, 5, 6))
            dense()
            mixer(1)
            norm_scale(3)
            route()
            experts()
            dve.wait_ge(gain_in, 32)
            for t in range(NT):
                one = slice(t, t + 1)
                dve.wait_ge(sumsq_done, 17 + t)
                v.tensor_scalar(ss[:, one], ss[:, one], 1.0 / D, EPS, ALU.mult, ALU.add).then_inc(ms_done, 1)
                dve.wait_ge(std_done, 5 + t)
                link(v.reciprocal(rstd[:, one], std[:, one]))
                v.scalar_tensor_tensor(out=xn[:, t, :], in0=x[:, t, :], scalar=rstd[:, t:t + 1],
                                       in1=gain_rows[:, :], op0=ALU.mult, op1=ALU.mult).then_inc(final_done, 1)

        @block.tensor
        def _(pe):
            mm, tr = nc.tensor.matmul, nc.tensor.transpose

            def transposed_norm(n, banks):
                for b in range(4):
                    for t in range(NT):
                        if b == 0:
                            pe.wait_ge(xn_done, NT * n + t + 1)
                        for k in (2 * b, 2 * b + 1):
                            c = (k % 2) * 256 + t * P
                            ins = tr(bank[banks[b]][:, c:c + P], xn[:, t, k:D:KT], ident[:, :])
                    ins.then_inc(xT_done, 1)

            def three(out, ah, al, wh, wl, start, stop, **kw):
                mm(out, ah, wh, start=start, stop=False, **kw)
                mm(out, ah, wl, start=False, stop=False, **kw)
                return mm(out, al, wh, start=False, stop=stop, **kw)

            def mix_pieces(layer, name, banks, q0, q1):
                wide, kk = (256, 4) if name == "kv" else (512, 2)
                for q in range(q0, q1):
                    n = MIX_BASE[layer] + MIX_FIRST[name] + q
                    r = n % RING
                    pe.wait_ge(lo_done, n + 1)
                    for i in range(kk):
                        k = kk * q + i
                        if name == "q":
                            pe.wait_ge(xTlo_done, 2 * KT * layer + k + 1)
                        elif name == "out0":
                            pe.wait_ge(mixlo_done, KT * layer + k + 1)
                        c = slice(i * wide, (i + 1) * wide)
                        for t in range(NT):
                            tt = slice(t * P, (t + 1) * P)
                            ins = three(bank[banks[t]][:, 0:wide], act_hi[:, k, tt], act_lo[:, k, tt],
                                        hi[:, r, c], lo[:, r, c], k == 0, k == KT - 1)
                    ins.then_inc(piece_used, 1)

            def scores(layer, t):
                for b in range(4):
                    for i in range(2):
                        h = 2 * b + i
                        rows = slice(HD * (h // 4), HD * (h // 4) + HD)
                        ins = mm(bank[b][:, i * SEQ:(i + 1) * SEQ], qT[rows, h % 4, t * P:(t + 1) * P],
                                 kT[rows, :], start=True, stop=True)
                    ins.then_inc(scores_done, 1)

            def turn_probs(layer, t):
                for h in range(NH):
                    pe.wait_ge(exp_done, (NH + 1) * (2 * layer + t) + h + 1)
                    for kt in range(NT):
                        c = (h % 2) * 256 + kt * P
                        ins = tr(bank[h // 2][:, c:c + P], prob[:, h * 256 + kt * P:h * 256 + kt * P + P], ident[:, :])
                ins.then_inc(probT_done, 1)

            def values(layer, t):
                i = 2 * (2 * layer + t + 1)
                pe.wait_ge(probT_out_a, i)
                pe.wait_ge(probT_out_v, i)
                for h in range(NH):
                    g = AW + KVW + HD * (h // (NH // NKV))
                    for kt in range(NT):
                        ins = mm(bank[6 + t][:, h * HD:(h + 1) * HD], probT[:, h * 256 + kt * P:h * 256 + kt * P + P],
                                 qkv[:, kt, g:g + HD], start=kt == 0, stop=kt == 1)
                ins.then_inc(av_done, 1)

            def mixer(layer):
                if layer == 0:
                    pe.wait_ge(ident_done, 1)
                transposed_norm(2 * layer, (0, 1, 2, 3))
                mix_pieces(layer, "q", (4, 5), 0, 4)
                mix_pieces(layer, "kv", (6, 7), 0, 2)
                pe.wait_ge(qkv_out, 4 * layer + 2)
                mix_pieces(layer, "c", (4, 5), 0, 4)
                pe.wait_ge(rope_done, layer + 1)
                for c in range(4):
                    for t in range(NT):
                        ins = tr(bank[c // 2][:, (c % 2) * 256 + t * P:(c % 2) * 256 + t * P + P],
                                 qkv[:, t, c * P:(c + 1) * P], ident[:, :])
                for t in range(NT):
                    ins = tr(bank[2][:, t * P:(t + 1) * P], qkv[:, t, AW:AW + KVW], ident[:, :])
                ins.then_inc(qkT_done, 1)
                pe.wait_ge(qkv_out, 4 * layer + 4)
                mix_pieces(layer, "u", (6, 7), 0, 2)
                pe.wait_ge(qT_out, 2 * (layer + 1))
                pe.wait_ge(kT_out, layer + 1)
                scores(layer, 0)
                mix_pieces(layer, "u", (6, 7), 2, 4)
                turn_probs(layer, 0)
                pe.wait_ge(c_out, 2 * (layer + 1))
                mix_pieces(layer, "b", (4, 5), 0, 2)
                pe.wait_ge(probT_out_a, 2 * (2 * layer + 1))
                pe.wait_ge(probT_out_v, 2 * (2 * layer + 1))
                scores(layer, 1)
                pe.wait_ge(z_done, 2 * (layer + 1))
                values(layer, 0)
                mix_pieces(layer, "b", (4, 5), 2, 4)
                turn_probs(layer, 1)
                pe.wait_ge(b_out, 2 * (layer + 1))
                for src, signal in ((z, zT_done), (bb, bT_done)):
                    if signal is bT_done:
                        pe.wait_ge(zT_out, 2 * (layer + 1))
                    for k in range(CT):
                        for t in range(NT):
                            c = (k % 2) * 256 + t * P
                            ins = tr(bank[4 + k // 2][:, c:c + P], src[:, t, k:CW:CT], ident[:, :])
                    ins.then_inc(signal, 1)
                values(layer, 1)
                if layer == 0:
                    pe.wait_ge(pool_done, POOL_STEPS)
                pe.wait_ge(sq_done, layer + 1)
                for k in range(CT):
                    ins = mm(bank[2][:, 0:SEQ], ones[:, :], sq[:, k, :], start=k == 0, stop=k == CT - 1)
                ins.then_inc(cms_done, 1)
                pe.wait_ge(attn_done, layer + 1)
                for k in range(4):
                    for t in range(NT):
                        c = (k % 2) * 256 + t * P
                        ins = tr(bank[k // 2][:, c:c + P], att[:, t, k:AW:4], ident[:, :])
                ins.then_inc(attT_done, 1)
                mix_pieces(layer, "out0", (4, 5), 0, 4)
                mix_pieces(layer, "out1", (6, 7), 0, 4)

            def gu_pieces(first, ring, tiles):
                for q in range(4):
                    pe.wait_ge(lo_done, first + q + 1)
                    r = (ring + q) % RING
                    for i in range(2):
                        k = 2 * q + i
                        c = slice(i * BLK, (i + 1) * BLK)
                        for b, tt in tiles:
                            ins = three(bank[b][:, :], act_hi[:, k, tt], act_lo[:, k, tt], hi[:, r, c], lo[:, r, c],
                                        k == 0, k == KT - 1)
                    ins.then_inc(piece_used, 1)

            def down_pieces(first, ring, tiles, last=False):
                for q in range(2):
                    pe.wait_ge(lo_done, first + q + 1)
                    r = (ring + q) % RING
                    for b, col, step in tiles:
                        tt = slice(col + q * step, col + q * step + P)
                        for c in range(2):
                            cc = slice(c * 512, (c + 1) * 512)
                            ins = three(bank[b + c][:, :], at_hi[:, tt], at_lo[:, tt], hi[:, r, cc], lo[:, r, cc],
                                        False, last and q == 1, skip_group_check=True)
                    ins.then_inc(piece_used, 1)

            def clear(banks):
                for b in banks:
                    ins = mm(bank[b][:, :], zeros[:, 0:P], zeros[:, :], start=True, stop=True)
                return ins

            def dense():
                b0 = DENSE_BASE
                tiles = [(t, slice(t * P, (t + 1) * P)) for t in range(NT)]
                outs = [(3 + 2 * t, t * P, NT * P) for t in range(NT)]

                def gu(h, first, ring):
                    if not isinstance(h, int) or h > 0:
                        pe.wait_ge(gated_done, h)
                    gu_pieces(first, ring, tiles)

                def turn(h, half):
                    pe.wait_ge(gated_done, h + 1)
                    if not isinstance(h, int) or h > 0:
                        pe.wait_ge(atTl_done, h)
                    for i in range(2):
                        for t in range(NT):
                            c = i * NT * P + t * P
                            ins = tr(bank[2][:, c:c + P], gated[:, 2 * half + t, i * P:(i + 1) * P], ident[:, :])
                    ins.then_inc(gT_done, 1)

                def down(h, first, ring, last=False):
                    pe.wait_ge(atTl_done, h + 1)
                    down_pieces(first, ring, outs, last)

                pe.wait_ge(xTlo_done, 2 * KT)
                gu(0, b0, b0)
                clear((3, 4, 5, 6))
                gu(1, b0 + 4, b0 + 4)
                turn(0, 0)
                with pe.Fori(0, 2) as i:
                    for j in (1, 2):
                        for half in range(2):
                            h = 4 * i + 2 * j + half
                            ring = b0 + gu_first(2 * j + half)
                            first = pe.snap(24 * i + ring)
                            gu(h, first, ring)
                            down(h - 2, first + 4, ring + 4)
                            turn(h - 1, 1 - half)
                h = DH - 1
                first = b0 + gu_first(h)
                gu(h, first, first)
                down(h - 2, first + 4, first + 4)
                turn(h - 1, 1)
                down(h - 1, first + 6, first + 6)
                turn(h, 0)
                down(h, first + 8, first + 8, last=True)

            def route():
                pe.wait_ge(routlo_done, 1)
                for k in range(KT):
                    pe.wait_ge(xTlo_done, 3 * KT + k + 1)
                    for part in (act_hi, act_lo):
                        ins = mm(bank[2][0:2 * NE, 0:SEQ], rout_hl[:, k, :], part[:, k, :],
                                 start=k == 0 and part is act_hi, stop=k == KT - 1 and part is act_lo)
                ins.then_inc(logT_done, 1)
                pe.wait_ge(logT_out, 1)
                for t in range(NT):
                    ins = tr(bank[7][:, t * 2 * NE:(t + 1) * 2 * NE], logT[:, t * P:(t + 1) * P],
                             ident[0:2 * NE, 0:2 * NE])
                ins.then_inc(logits_done, 1)
                pe.wait_ge(chosen_done, 1)
                r = bank[7]
                mm(r[:, 0:NE], before[:, :], chosen[:, 0, :], start=True, stop=True)
                mm(r[:, NE:2 * NE], ones[:, :], chosen[:, 0, :], start=True, stop=False)
                mm(r[:, NE:2 * NE], before[:, :], chosen[:, 1, :], start=False, stop=True)
                mm(r[:, 2 * NE:3 * NE], ones[:, :], chosen[:, 0, :], start=True, stop=False)
                mm(r[:, 2 * NE:3 * NE], ones[:, :], chosen[:, 1, :], start=False, stop=True).then_inc(rank_done, 1)

            def experts():
                b0 = MOE_BASE

                def gu(half, first, ring, n):
                    pe.wait_ge(gated_done, n - 1)
                    gu_pieces(first, ring, [(half, slice(0, P))])

                def turn(half, n):
                    pe.wait_ge(gated_done, n + 1)
                    pe.wait_ge(atTl_done, n)
                    for i in range(2):
                        c = half * 256 + i * P
                        ins = tr(bank[2][:, c:c + P], gated[:, half, i * P:(i + 1) * P], ident[:, :])
                    ins.then_inc(gT_done, 1)

                def down(half, first, ring, n, last=False):
                    pe.wait_ge(atTl_done, n + 1)
                    down_pieces(first, ring, [(3, half * 256, P)], last)

                def gather(p, ready=sel_done, done=gathered):
                    pe.wait_ge(ready, p)
                    for k in range(KT):
                        for t in range(NT):
                            ins = mm(bank[5 + k // 4][:, (k % 4) * P:(k % 4 + 1) * P], xn[:, t, k:D:KT], sel[:, t, :],
                                     start=t == 0, stop=t == 1)
                    ins.then_inc(done, 1)

                def scatter(p, added, done, banks=(5, 6, 7, 5)):
                    for r, b in enumerate(banks):
                        t, c = r // 2, r % 2
                        if b in banks[:r]:
                            pe.wait_ge(added, p)
                        mm(bank[b][:, :], gselT[:, t * P:(t + 1) * P], y[:, c * 512:(c + 1) * 512],
                           start=True, stop=True).then_inc(done, 1)

                def scatter_last(p):
                    pe.wait_ge(y_act, p + 1)
                    pe.wait_ge(y_dve, p + 1)
                    pe.wait_ge(gselT_out, p + 1)
                    scatter(12 + 4 * p + 1, x_changed, scattered)

                def turn_gates(p):
                    pe.wait_ge(gsel_done, p + 1)
                    for t in range(NT):
                        ins = tr(bank[7][:, t * P:(t + 1) * P], gsel[:, t, :], ident[:, :])
                    ins.then_inc(gselT_done, 1)

                def one_tile(p, first, n0):
                    pe.wait_ge(xelo_done, 2 * p + 2)
                    gu(0, first, b0, n0)
                    scatter_last(p)
                    clear((3, 4))
                    gu(1, first + 4, b0 + 4, n0 + 1)
                    turn(0, n0)
                    with pe.Fori(1, EB) as j:
                        f = pe.snap(first + 12 * j - 4)
                        n = pe.snap(n0 + 2 * j)
                        gu(0, f, b0 + 8, n)
                        down(0, f + 4, b0 + 12, n - 2)
                        turn(1, n - 1)
                        gu(1, f + 6, b0 + 14, n + 1)
                        down(1, f + 10, b0 + 18, n - 1)
                        turn(0, n)
                    f = pe.snap(first + d_first(EH - 2, EH))
                    n = pe.snap(n0 + EH)
                    pe.wait_ge(x_changed, 12 + 4 * (p + 1))
                    gather(p + 2)
                    turn_gates(p)
                    turn(1, n - 1)
                    down(0, f, b0 + 8, n - 2)
                    down(1, f + 2, b0 + 10, n - 1, last=True)

                def two_tiles(p, first, n0, u):
                    tiles = [(t, slice(t * P, (t + 1) * P)) for t in range(NT)]
                    outs = [(3 + 2 * t, t * P, NT * P) for t in range(NT)]

                    def gu_both(n, first, ring):
                        pe.wait_ge(gated_done, n)
                        gu_pieces(first, ring, tiles)

                    def turn_both(n, half):
                        pe.wait_ge(gated_done, n + 1)
                        pe.wait_ge(atTl_done, n)
                        for i in range(2):
                            for t in range(NT):
                                c = i * NT * P + t * P
                                ins = tr(bank[2][:, c:c + P], gated[:, 2 * half + t, i * P:(i + 1) * P], ident[:, :])
                        ins.then_inc(gT_done, 1)

                    def down_both(n, first, ring, last=False):
                        pe.wait_ge(atTl_done, n + 1)
                        down_pieces(first, ring, outs, last)

                    pe.wait_ge(xelo_done, 2 * p + 2)
                    gather(u + 1, sel2_done, gathered2)
                    pe.wait_ge(xelo2_done, 2 * u + 2)
                    gu_both(n0, first, b0)
                    scatter_last(p)
                    gu_both(n0 + 1, first + 4, b0 + 4)
                    pe.wait_ge(x_changed, 12 + 4 * (p + 1))
                    clear((3, 4, 5, 6))
                    turn_both(n0, 0)
                    with pe.Fori(1, EB) as j:
                        f = pe.snap(first + 12 * j - 4)
                        n = pe.snap(n0 + 2 * j)
                        for half in range(2):
                            gu_both(n + half, f + 6 * half, b0 + 8 + 6 * half)
                            down_both(n + half - 2, f + 6 * half + 4, b0 + 12 + 6 * half)
                            turn_both(n + half - 1, 1 - half)
                    f = pe.snap(first + d_first(EH - 2, EH))
                    n = pe.snap(n0 + EH)
                    pe.wait_ge(gsel2_done, u + 1)
                    for t in range(NT):
                        ins = tr(bank[7][:, t * P:(t + 1) * P], gsel2[:, t, :], ident[:, :])
                    ins.then_inc(gselT2_done, 1)
                    down_both(n - 2, f, b0 + 8)
                    turn_both(n - 1, 1)
                    down_both(n - 1, f + 2, b0 + 10, last=True)
                    pe.wait_ge(y2_act, u + 1)
                    pe.wait_ge(y2_dve, u + 1)
                    pe.wait_ge(gselT2_out, u + 1)
                    scatter(4 * u + 1, x_changed2, scattered2, (0, 1, 2, 7))
                    gather(p + 2)
                    pe.wait_ge(x_changed2, 4 * u + 4)
                    turn_gates(p)

                pe.wait_ge(plan_done, 1)
                code = pe.value_load(plan[0:1, 0:1], min_val=0, max_val=65535)
                pe.wait_ge(xg_done, 2)
                clear((3, 4)).then_inc(scattered, 1)
                gather(1)
                with pe.Fori(0, NE) as p:
                    first = pe.snap(b0 + E_PIECES * p)
                    n0 = pe.snap(DH + EH * p)
                    v = pe.snap((code >> (2 * p)) & 3, min_val=0, max_val=3)
                    with pe.If(v > 0):
                        two_tiles(p, first, n0, pe.snap((v + 3) & 3, min_val=0, max_val=3))
                    with pe.Else():
                        one_tile(p, first, n0)
                scatter_last(NE)

            mixer(0)
            transposed_norm(1, (3, 4, 5, 6))
            dense()
            mixer(1)
            transposed_norm(3, (3, 4, 5, 6))
            route()
            experts()


_INS = ["x", "positions", "mix_norm_g", "w_in", "conv_w", "sink", "att_out_g", "conv_out_g", "w_out",
        "ffn_norm_g", "dense_w_gate", "dense_w_up", "dense_w_down", "router_w",
        "moe_w_gate", "moe_w_up", "moe_w_down", "final_norm_g"]


def kernel(**inputs):
    import concourse.bacc as bacc
    from concourse.bass_utils import run_bass_kernel_spmd

    nc = bacc.Bacc("TRN2", target_bir_lowering=False, num_devices=1)
    arrays, args = {}, []
    for name in _INS:
        a = np.ascontiguousarray(inputs[name])
        arrays[f"in_{name}"] = a
        args.append(nc.dram_tensor(f"in_{name}", a.shape, mybir.dt.from_np(a.dtype), kind="ExternalInput").ap())
    out = nc.dram_tensor("out", (1, SEQ, D), F32, kind="ExternalOutput").ap()
    build_trunk(nc, *args, out)
    return run_bass_kernel_spmd(nc, [arrays], core_ids=[0]).results[0]["out"]
```
